# Optimizing a Trainium2 kernel written in Bass

```python
import math
import jax, jax.numpy as jnp
from jax import lax
import numpy as np

D_MODEL = 2048
BATCH = 1
SEQ = 256
DEPTH = 1

NSA_HEADS = 16
NSA_KV_GROUPS = 4
NSA_HEAD_DIM = 128
CMP_BLOCK = 32
CMP_STRIDE = 16
SEL_BLOCK = 64
SEL_TOPK = 16
WINDOW = 512
Q_BLOCK = 128
ROPE_THETA = 10000.0
FORCED_SCORE = 1.0e4
SSM_EXPAND = 2
SSM_D_INNER = SSM_EXPAND * D_MODEL
SSM_HEAD_DIM = 64
SSM_HEADS = SSM_D_INNER // SSM_HEAD_DIM
SSM_GROUPS = 8
SSM_STATE = 128
CONV_WIDTH = 4
SSD_CHUNK = 128
XBC_W = SSM_D_INNER + 2 * SSM_GROUPS * SSM_STATE
D_FF = 4 * D_MODEL
EPS = 1e-6
NEG_INF = -1e30
TINY = 1e-30

Q_W = NSA_HEADS * NSA_HEAD_DIM
KV_W = NSA_KV_GROUPS * NSA_HEAD_DIM
NSA_GATE_W = 3 * NSA_HEADS
IN_SIZES = (Q_W, KV_W, KV_W, KV_W, KV_W, KV_W, KV_W, NSA_GATE_W,
            SSM_D_INNER, XBC_W, SSM_HEADS, 2 * D_MODEL)
IN_W = sum(IN_SIZES)

kernel_name = "nsa_mamba2_gated_hybrid_block"

def _split_points():
    points, acc = [], 0
    for s in IN_SIZES[:-1]:
        acc += s
        points.append(acc)
    return points

def rms_norm(x, w):
    xf = x.astype(jnp.float32)
    y = xf * lax.rsqrt(jnp.mean(xf * xf, axis=-1, keepdims=True) + EPS)
    return (y * w.astype(jnp.float32)).astype(x.dtype)

def rope_tables(positions, dim):
    inv = ROPE_THETA ** (-jnp.arange(0, dim, 2, dtype=jnp.float32) / dim)
    ang = positions.astype(jnp.float32)[..., None] * inv
    return jnp.cos(ang), jnp.sin(ang)

def apply_rope(x, cos, sin):
    x1, x2 = jnp.split(x.astype(jnp.float32), 2, axis=-1)
    c, s = cos[:, :, None, :], sin[:, :, None, :]
    return jnp.concatenate([x1 * c - x2 * s, x2 * c + x1 * s], axis=-1).astype(x.dtype)

def masked_softmax(s, mask):
    s = jnp.where(mask, s.astype(jnp.float32), NEG_INF)
    m = jnp.max(s, axis=-1, keepdims=True)
    p = jnp.exp(s - m) * mask
    return p / jnp.maximum(jnp.sum(p, axis=-1, keepdims=True), TINY)

def nsa_mixer(q, k_c, v_c, k_s, v_s, k_w, v_w, gate_logits, cos, sin,
              cmp_pos_k, cmp_pos_v, cmp_k_w1, cmp_k_w2, cmp_v_w1, cmp_v_w2):
    Bsz, S = q.shape[:2]
    G, R, Dh = NSA_KV_GROUPS, NSA_HEADS // NSA_KV_GROUPS, NSA_HEAD_DIM
    scale = Dh ** -0.5
    t = jnp.arange(S)
    nb = S // Q_BLOCK

    q = apply_rope(q.reshape(Bsz, S, NSA_HEADS, Dh), cos, sin)
    q = q.reshape(Bsz, S, G, R, Dh).transpose(0, 2, 3, 1, 4)

    n_cmp = (S - CMP_BLOCK) // CMP_STRIDE + 1
    cmp_idx = jnp.arange(n_cmp)[:, None] * CMP_STRIDE + jnp.arange(CMP_BLOCK)[None, :]
    cmp_end = cmp_idx[:, -1]

    def compress(kv, pos_emb, w1, w2):
        blocks = kv.reshape(Bsz, S, G, Dh)[:, cmp_idx] + pos_emb[:, None, :]
        flat = blocks.transpose(0, 1, 3, 2, 4).reshape(Bsz, n_cmp, G, CMP_BLOCK * Dh)
        return jax.nn.silu(flat @ w1) @ w2

    kc = apply_rope(compress(k_c, cmp_pos_k, cmp_k_w1, cmp_k_w2), cos[:, cmp_end], sin[:, cmp_end])
    kc = kc.transpose(0, 2, 1, 3)
    vc = compress(v_c, cmp_pos_v, cmp_v_w1, cmp_v_w2).transpose(0, 2, 1, 3)
    s_c = jnp.einsum('bgrsd,bgcd->bgrsc', q, kc) * scale
    p_c = masked_softmax(s_c, cmp_end[None, :] <= t[:, None])
    o_c = jnp.einsum('bgrsc,bgcd->bgrsd', p_c.astype(vc.dtype), vc)

    n_sel = S // SEL_BLOCK
    k_top = min(SEL_TOPK, n_sel)
    c_start = jnp.arange(n_cmp) * CMP_STRIDE
    s_start = jnp.arange(n_sel) * SEL_BLOCK
    overlap = jnp.clip(jnp.minimum(c_start[:, None] + CMP_BLOCK, s_start[None, :] + SEL_BLOCK)
                       - jnp.maximum(c_start[:, None], s_start[None, :]), 0, None)
    cmp_to_sel = (overlap / CMP_STRIDE).astype(jnp.float32)
    imp = jnp.einsum('bgrsc,cn->bgsn', p_c, cmp_to_sel)
    cur = t // SEL_BLOCK
    j = jnp.arange(n_sel)
    forced = (j[None, :] == 0) | (j[None, :] == cur[:, None]) | (j[None, :] == cur[:, None] - 1)
    future = j[None, :] > cur[:, None]
    imp = jnp.where(future, -1.0, jnp.where(forced, FORCED_SCORE, imp))
    _, sel_idx = lax.top_k(imp, k_top)

    k_s = apply_rope(k_s.reshape(Bsz, S, G, Dh), cos, sin)
    ks_blocks = k_s.transpose(0, 2, 1, 3).reshape(Bsz, G, n_sel, SEL_BLOCK, Dh)
    vs_blocks = v_s.reshape(Bsz, S, G, Dh).transpose(0, 2, 1, 3).reshape(Bsz, G, n_sel, SEL_BLOCK, Dh)
    q_blk = q.reshape(Bsz, G, R, nb, Q_BLOCK, Dh)
    gather = jax.vmap(jax.vmap(lambda blocks, idx: blocks[idx]))
    n_keys = k_top * SEL_BLOCK

    def sel_block(args):
        qb, ib, tb = args
        kg = gather(ks_blocks, ib).reshape(Bsz, G, Q_BLOCK, n_keys, Dh)
        vg = gather(vs_blocks, ib).reshape(Bsz, G, Q_BLOCK, n_keys, Dh)
        s = jnp.einsum('bgrqd,bgqnd->bgrqn', qb, kg) * scale
        kpos = (ib[..., None] * SEL_BLOCK + jnp.arange(SEL_BLOCK)).reshape(Bsz, G, Q_BLOCK, n_keys)
        mask = (kpos <= tb[:, None])[:, :, None]
        p = masked_softmax(s, mask)
        return jnp.einsum('bgrqn,bgqnd->bgrqd', p.astype(vg.dtype), vg)

    o_s = lax.map(sel_block, (jnp.moveaxis(q_blk, 3, 0),
                              jnp.moveaxis(sel_idx.reshape(Bsz, G, nb, Q_BLOCK, k_top), 2, 0),
                              t.reshape(nb, Q_BLOCK)))
    o_s = jnp.moveaxis(o_s, 0, 3).reshape(Bsz, G, R, S, Dh)

    k_w = apply_rope(k_w.reshape(Bsz, S, G, Dh), cos, sin).transpose(0, 2, 1, 3)
    v_w = v_w.reshape(Bsz, S, G, Dh).transpose(0, 2, 1, 3)
    span = WINDOW + Q_BLOCK
    win_idx = jnp.arange(nb)[:, None] * Q_BLOCK + jnp.arange(span)[None, :]
    pad = ((0, 0), (0, 0), (WINDOW, 0), (0, 0))
    kw = jnp.pad(k_w, pad)[:, :, win_idx]
    vw = jnp.pad(v_w, pad)[:, :, win_idx]
    kpos = win_idx - WINDOW
    diff = t.reshape(nb, Q_BLOCK)[:, :, None] - kpos[:, None, :]
    wmask = (diff >= 0) & (diff < WINDOW) & (kpos[:, None, :] >= 0)
    s_w = jnp.einsum('bgrnqd,bgnkd->bgrnqk', q_blk, kw) * scale
    p_w = masked_softmax(s_w, wmask)
    o_w = jnp.einsum('bgrnqk,bgnkd->bgrnqd', p_w.astype(vw.dtype), vw).reshape(Bsz, G, R, S, Dh)

    def to_heads(o):
        return o.transpose(0, 3, 1, 2, 4).reshape(Bsz, S, NSA_HEADS, Dh)

    g = jax.nn.sigmoid(gate_logits.reshape(Bsz, S, NSA_HEADS, 3))
    o = g[..., 0:1] * to_heads(o_c) + g[..., 1:2] * to_heads(o_s) + g[..., 2:3] * to_heads(o_w)
    return o.reshape(Bsz, S, Q_W)

def ssd_chunked(xdt, a, bm, cm):
    Bsz, S, H, P = xdt.shape
    G, N = bm.shape[2], bm.shape[3]
    R = H // G
    L = SSD_CHUNK
    C = S // L
    x = xdt.reshape(Bsz, C, L, G, R, P)
    a = a.astype(jnp.float32).reshape(Bsz, C, L, G, R).transpose(0, 3, 4, 1, 2)
    bm = bm.reshape(Bsz, C, L, G, N)
    cm = cm.reshape(Bsz, C, L, G, N)
    a_cs = jnp.cumsum(a, axis=-1)
    causal = jnp.tril(jnp.ones((L, L), dtype=bool))
    seg = a_cs[..., :, None] - a_cs[..., None, :]
    decay = jnp.exp(jnp.where(causal, seg, -jnp.inf))
    cb = jnp.einsum('bclgn,bcsgn->bgcls', cm, bm)
    y_diag = jnp.einsum('bgcls,bgrcls,bcsgrp->bclgrp', cb, decay, x)
    decay_states = jnp.exp(a_cs[..., -1:] - a_cs)
    states = jnp.einsum('bclgn,bgrcl,bclgrp->bcgrpn', bm, decay_states, x).astype(jnp.float32)
    chunk_decay = jnp.exp(a_cs[..., -1])

    def step(h, inp):
        st, dec = inp
        return h * dec[..., None, None] + st, h

    h0 = jnp.zeros((Bsz, G, R, P, N), jnp.float32)
    _, prev = lax.scan(step, h0, (jnp.moveaxis(states, 1, 0), jnp.moveaxis(chunk_decay, 3, 0)))
    prev = jnp.moveaxis(prev, 0, 1)
    y_off = jnp.einsum('bclgn,bcgrpn,bgrcl->bclgrp', cm, prev, jnp.exp(a_cs))
    return (y_diag + y_off).reshape(Bsz, S, H, P).astype(xdt.dtype)

def mamba2_mixer(z, xbc, dt_raw, conv_w, conv_b, dt_bias, a_log, ssm_d, ssm_norm_w):
    Bsz, S = z.shape[:2]
    xbc = lax.conv_general_dilated(xbc, conv_w[:, None, :], window_strides=(1,),
                                   padding=[(CONV_WIDTH - 1, 0)],
                                   dimension_numbers=('NWC', 'WIO', 'NWC'),
                                   feature_group_count=XBC_W)
    xbc = jax.nn.silu(xbc + conv_b)
    xs, bm, cm = jnp.split(xbc, [SSM_D_INNER, SSM_D_INNER + SSM_GROUPS * SSM_STATE], axis=-1)
    xs = xs.reshape(Bsz, S, SSM_HEADS, SSM_HEAD_DIM)
    bm = bm.reshape(Bsz, S, SSM_GROUPS, SSM_STATE)
    cm = cm.reshape(Bsz, S, SSM_GROUPS, SSM_STATE)
    dt = jax.nn.softplus(dt_raw.astype(jnp.float32) + dt_bias.astype(jnp.float32))
    a = -jnp.exp(a_log.astype(jnp.float32))
    y = ssd_chunked(xs * dt[..., None].astype(xs.dtype), dt * a, bm, cm)
    y = y + ssm_d[:, None] * xs
    y = y.reshape(Bsz, S, SSM_D_INNER) * jax.nn.silu(z)
    yg = y.reshape(Bsz, S, SSM_GROUPS, SSM_D_INNER // SSM_GROUPS).astype(jnp.float32)
    yg = yg * lax.rsqrt(jnp.mean(yg * yg, axis=-1, keepdims=True) + EPS)
    return (yg.reshape(Bsz, S, SSM_D_INNER) * ssm_norm_w.astype(jnp.float32)).astype(z.dtype)

def setup_inputs(seed: int = 0) -> dict:
    key = jax.random.key(seed)
    ks = jax.random.split(key, 24)
    f32 = jnp.float32
    L = DEPTH

    def nrm(k, shape, fan_in):
        return jax.random.normal(k, shape, f32) * fan_in ** -0.5

    def gain(k, shape):
        return 1.0 + 0.02 * jax.random.normal(k, shape, f32)

    x = jax.random.normal(ks[0], (BATCH, SEQ, D_MODEL), f32)
    offset = jax.random.randint(ks[1], (BATCH, 1), 0, 1024, jnp.int32)
    positions = jnp.arange(SEQ, dtype=jnp.int32)[None, :] + offset
    dt0 = jnp.exp(jax.random.uniform(ks[12], (L, SSM_HEADS), f32, math.log(1e-3), math.log(1e-1)))
    return {
        "x": x,
        "positions": positions,
        "norm_mix_w": gain(ks[2], (L, D_MODEL)),
        "w_in": nrm(ks[3], (L, D_MODEL, IN_W), D_MODEL),
        "cmp_pos_k": 0.02 * jax.random.normal(ks[4], (L, CMP_BLOCK, NSA_HEAD_DIM), f32),
        "cmp_pos_v": 0.02 * jax.random.normal(ks[5], (L, CMP_BLOCK, NSA_HEAD_DIM), f32),
        "cmp_k_w1": nrm(ks[6], (L, CMP_BLOCK * NSA_HEAD_DIM, NSA_HEAD_DIM), CMP_BLOCK * NSA_HEAD_DIM),
        "cmp_k_w2": nrm(ks[7], (L, NSA_HEAD_DIM, NSA_HEAD_DIM), NSA_HEAD_DIM),
        "cmp_v_w1": nrm(ks[8], (L, CMP_BLOCK * NSA_HEAD_DIM, NSA_HEAD_DIM), CMP_BLOCK * NSA_HEAD_DIM),
        "cmp_v_w2": nrm(ks[9], (L, NSA_HEAD_DIM, NSA_HEAD_DIM), NSA_HEAD_DIM),
        "conv_w": nrm(ks[10], (L, CONV_WIDTH, XBC_W), CONV_WIDTH),
        "conv_b": 0.01 * jax.random.normal(ks[11], (L, XBC_W), f32),
        "dt_bias": dt0 + jnp.log(-jnp.expm1(-dt0)),
        "a_log": jnp.log(jax.random.uniform(ks[13], (L, SSM_HEADS), f32, 1.0, 16.0)),
        "ssm_d": 1.0 + 0.1 * jax.random.normal(ks[14], (L, SSM_HEADS), f32),
        "ssm_norm_w": gain(ks[15], (L, SSM_D_INNER)),
        "w_proj_nsa": nrm(ks[16], (L, Q_W, D_MODEL), Q_W),
        "w_proj_ssm": nrm(ks[17], (L, SSM_D_INNER, D_MODEL), SSM_D_INNER),
        "w_out": nrm(ks[18], (L, D_MODEL, D_MODEL), D_MODEL),
        "norm_mlp_w": gain(ks[19], (L, D_MODEL)),
        "w_up": nrm(ks[20], (L, D_MODEL, D_FF), D_MODEL),
        "w_down": nrm(ks[21], (L, D_FF, D_MODEL), D_FF),
        "norm_final_w": gain(ks[22], (D_MODEL,)),
    }

def reference(x, positions, norm_mix_w, w_in, cmp_pos_k, cmp_pos_v, cmp_k_w1, cmp_k_w2,
              cmp_v_w1, cmp_v_w2, conv_w, conv_b, dt_bias, a_log, ssm_d, ssm_norm_w,
              w_proj_nsa, w_proj_ssm, w_out, norm_mlp_w, w_up, w_down, norm_final_w):
    cos, sin = rope_tables(positions, NSA_HEAD_DIM)
    split_points = _split_points()
    h = x
    for l in range(DEPTH):
        u = rms_norm(h, norm_mix_w[l])
        proj = u @ w_in[l]
        (q, k_c, v_c, k_s, v_s, k_w, v_w, nsa_gate, z, xbc, dt_raw,
         branch_gate) = jnp.split(proj, split_points, axis=-1)
        o_nsa = nsa_mixer(q, k_c, v_c, k_s, v_s, k_w, v_w, nsa_gate, cos, sin,
                          cmp_pos_k[l], cmp_pos_v[l], cmp_k_w1[l], cmp_k_w2[l],
                          cmp_v_w1[l], cmp_v_w2[l])
        o_ssm = mamba2_mixer(z, xbc, dt_raw, conv_w[l], conv_b[l], dt_bias[l], a_log[l],
                             ssm_d[l], ssm_norm_w[l])
        gate_a, gate_b = jnp.split(branch_gate, 2, axis=-1)
        merged = (jax.nn.sigmoid(gate_a) * (o_nsa @ w_proj_nsa[l])
                  + jax.nn.sigmoid(gate_b) * (o_ssm @ w_proj_ssm[l]))
        h = h + merged @ w_out[l]
        hn = rms_norm(h, norm_mlp_w[l])
        h = h + jnp.square(jax.nn.relu(hn @ w_up[l])) @ w_down[l]
    return rms_norm(h, norm_final_w)


_drawn_inputs = setup_inputs


def setup_inputs(seed=0):
    import zlib

    import numpy as np

    out = dict(_drawn_inputs(seed))
    spreads = {}
    factors = {'norm_mix_w': 3.403,
     'cmp_pos_k': 87.499,
     'cmp_pos_v': 39.803,
     'conv_b': 8.0,
     'ssm_norm_w': 16.055,
     'norm_mlp_w': 10.65,
     'norm_final_w': 22.898,
     'ssm_d': 45.034}
    for name, (base, spread) in spreads.items():
        noise = np.random.default_rng([zlib.crc32(name.encode()), seed]).standard_normal(out[name].shape)
        drawn = base * np.exp(spread * noise) if base else spread * noise
        out[name] = __import__('jax').numpy.asarray(drawn.astype(out[name].dtype))
    for name, factor in factors.items():
        out[name] = (out[name] * factor).astype(out[name].dtype)
    return out
```

```python
from contextlib import ExitStack

import numpy as np

import concourse.bass as bass
from concourse import mybir

F32 = mybir.dt.float32
F32R = mybir.dt.float32r
BF16 = mybir.dt.bfloat16
I32 = mybir.dt.int32
ALU = mybir.AluOpType
ACT = mybir.ActivationFunctionType
AX = mybir.AxisListType
ds = bass.ds

P = 128
S = 256
D = 2048
HD = 128
NH = 16
NG = 4
CMP, STR = 32, 16
NCMP = (S - CMP) // STR + 1
SCALE = float(HD) ** -0.5
NEG = -1e30
TINY = 1e-30
EPS = 1e-6
SG = 8
SH = 64
DI = 4096
XBCW = DI + 2 * SG * P
NC = 512
KT = 16
RING = 4
LEAD = 3
KC0, VC0, KS0, VS0, KW0, VW0 = (D + NC * i for i in range(6))
NG0 = D + 6 * NC
Z0 = NG0 + 3 * NH
XBC0 = Z0 + DI
DT0 = XBC0 + XBCW
GATE0 = DT0 + SH
SMALL = 3 * NH + SH
CN1, CSN, CN2, CCB, CCW, CPK, CPV = 0, 16, 48, 64, 112, 304, 336
C_SMALL, C_KC, C_VC, C_KS, C_VS, C_KW, C_VW, C_AT = 0, 1, 2, 3, 4, 5, 6, 7
C_PA = C_AT + 16
C_X0 = C_PA + 4
C_L1 = C_X0 + 2
C_PB1 = C_L1 + 8
C_L2 = C_PB1 + 4
C_PB2 = C_L2 + 6
C_WO = C_PB2 + 4
C_MLP = C_WO + 4
C_END = C_MLP + 32
E_U, E_KC, E_VC, E_KS, E_KW, E_AT = 0, 4, 5, 6, 7, 8
PER_AT = 10
EQ, EBC = 0, 3
EPT = (1, 4, 6, 8)
EPV = (2, 5, 7, 9)
E_X0 = E_AT + 4 * PER_AT
E_L1 = E_X0 + 2
E_L2 = E_L1 + 8
E_PB2 = E_L2 + 6
E_WO = E_PB2 + 4
E_MLP = E_WO + 4
SL_S, SL_PT, SL_PV = (12, 17, 22, 25), (15, 22, 25, 28), (17, 24, 27, 30)
SL_Q, SL_BC = 10, 19

N_SMALL = 17
XA_X0 = C_PA
XA_UP = XA_X0 + 16
SS_WO = 2 + 2 * SG + 8


def build(nc, a, out):
    ctx = ExitStack()
    with ctx:
        def sb(name, shape, dt=F32, c=ctx):
            return c.enter_context(nc.sbuf_tensor(name, shape, dt))

        def sem(name):
            return ctx.enter_context(nc.semaphore(name))

        acc = [[ctx.enter_context(nc.psum_tensor(f"acc{i}{t}", [P, NC], F32)) for t in range(2)] for i in range(2)]
        TR = [ctx.enter_context(nc.psum_tensor(f"tr{b}", [P, NC], F32)) for b in range(2)]
        X6 = ctx.enter_context(nc.psum_tensor("x6", [P, NC], F32))
        X7 = ctx.enter_context(nc.psum_tensor("x7", [P, NC], F32))

        raw = sb("raw", [P, RING, 2, NC])
        hi = sb("hi", [P, RING, 2, NC], F32R)
        lo = sb("lo", [P, RING, 2, NC], F32R)
        LAh = sb("LAh", [P, KT, S], F32R)
        LAl = sb("LAl", [P, KT, S], F32R)
        LBh = sb("LBh", [P, KT, S], F32R)
        LBl = sb("LBl", [P, KT, S], F32R)
        GA = sb("GA", [P, 2, D])
        GB = sb("GB", [P, 2, D])
        BCT = sb("BCT", [P, KT, S])
        H = BCT[:, :, :].rearrange("p a b -> p (a b)").rearrange("p (t n) -> p t n", t=2)
        XR = sb("XR", [P, 2, NC])
        Y = sb("Y", [P, 2, NC])
        COLS = sb("COLS", [P, 368])
        identf = sb("identf", [P, P])
        identb = sb("identb", [P, P], BF16)
        tri = sb("tri", [P, P])
        ones = sb("ones", [P, P])
        maskq = sb("maskq", [P, P], BF16)
        maskt = sb("maskt", [P, P], BF16)
        DT = sb("DT", [P, 2, SH])
        DA = sb("DA", [P, 2, SH])
        ACS = sb("ACS", [P, 2, SH])
        DST = sb("DST", [P, SH])
        EA1 = sb("EA1", [P, SH])
        DBC = sb("DBC", [P, SH])
        GR = sb("GR", [P, NH, 6])
        CWs = sb("CWs", [P, 5, 4])
        SS = sb("SS", [P, 16])
        SS2 = sb("SS2", [P, 2, 4])
        VV = sb("VV", [P, 4])
        RS = sb("RS", [P, 4])
        mhalf = sb("mhalf", [P, 4])

        s_raw = [sem(f"raw{i}") for i in range(RING)]
        s_hi = sem("hi_done")
        s_lo = sem("lo_done")
        s_mm = sem("group_multiplied")
        s_acc = sem("chunk_evacuated")
        s_xa = sem("act_half_evacuated")
        s_tr = sem("bank_transposed")
        s_tra = sem("event_read_by_act")
        s_trd = sem("event_read_by_dve")
        s_x = sem("x_landed")
        s_small = sem("small_landed")
        s_const = sem("constants_made")
        s_cdve = sem("constants_made_dve")
        s_w12 = sem("compression_weights_landed")
        s_colp = sem("cols_transposed")
        s_colc = sem("cols_copied")
        s_ss = sem("squares_summed")
        s_v = sem("variance_ready")
        s_pow = sem("rsqrt_ready")
        s_u = sem("u_ready")
        s_ang = sem("angles_ready")
        s_sin = sem("sines_ready")
        s_dts = sem("dt_steps_dve")
        s_dta = sem("dt_steps_act")
        s_acs = sem("cumulative_sums")
        s_rope = sem("rotated")
        s_xp = sem("compression_blocks_ready")
        s_hid = sem("compression_products")
        s_hta = sem("compression_tanh")
        s_hs = sem("compression_hidden_ready")
        s_kcr = sem("compressed_key_rotated")
        s_vcd = sem("compressed_values_copied")
        s_stage = sem("attention_operands_staged")
        s_sc = sem("scores_ready")
        s_nm = sem("maxima_ready")
        s_ex = sem("exponentials_ready")
        s_p = sem("probabilities_scaled")
        s_gt = sem("gate_tanh_ready")
        s_cw = sem("conv_weights_staged")
        s_ct = sem("conv_tanh_done")
        s_xs = sem("conv_output_ready")
        s_pg = sem("scan_operands_staged")
        s_xt = sem("xs_in_token_rows")
        s_xd = sem("scan_inputs_ready")
        s_xdd = sem("skip_term_ready")
        s_cb = sem("cb_products")
        s_cbc = sem("cb_copied")
        s_dk = sem("decay_sums")
        s_sub = sem("decay_exponent_ready")
        s_dx = sem("decay_ready")
        s_w = sem("scan_weights_ready")
        s_st = sem("state_product")
        s_stc = sem("state_copied")
        s_y0 = sem("first_chunk_product")
        s_y0d = sem("first_chunk_read")
        s_ey = sem("second_chunk_products")
        s_zt = sem("z_tanh_ready")
        s_yg = sem("gated_y_ready")
        s_yn = sem("normed_y_ready")
        s_e3 = sem("y_transposed")
        s_e3a = sem("y_read_by_act")
        s_e3d = sem("y_read_by_dve")
        s_mg = sem("merged_ready")
        s_hr = sem("residual_landed")
        s_h = sem("residual_added")
        s_ff = sem("mlp_rows_ready")
        s_fin = sem("output_ready")
        s_wf = sem("final_weights_landed")
        s_out = sem("output_stored")

        w_in = a["w_in"].rearrange("(k p) c -> p k c", p=P)

        def load_chunk(sp, C, w, k0, c0, n=NC, extra=None):
            for j in range(8):
                sl = j % RING
                if not (isinstance(C, int) and 8 * C + j < RING):
                    sp.wait_ge(s_lo, 8 * C + j - RING + 1)
                for (src, cc, dst, m) in extra or [(w, c0, 0, n)]:
                    x = sp.dma_start(raw[:, sl, :, dst:dst + m], src[:, ds(k0 + 2 * j, 2), ds(cc, m)])
                    x.then_inc(s_raw[sl], 16)

        def split_hi(act, C, j):
            n = SMALL if isinstance(C, int) and C == 0 else NC
            sl = j % RING
            if isinstance(C, int) and C == 0:
                act.wait_ge(s_raw[sl], 32 * (j // RING + 1))
            else:
                act.wait_ge(s_raw[sl], 16 * (2 * C + j // RING + 1) + 32)
            if not (isinstance(C, int) and 8 * C + j < RING):
                act.wait_ge(s_mm, 8 * C + j - RING + 1)
            act.activation(hi[:, sl, :, 0:n], raw[:, sl, :, 0:n], ACT.Copy).then_inc(s_hi, 1)

        def split_lo(dve, C, j):
            n = SMALL if isinstance(C, int) and C == 0 else NC
            sl = j % RING
            dve.wait_ge(s_hi, 8 * C + j + 1)
            dve.tensor_tensor(lo[:, sl, :, 0:n], raw[:, sl, :, 0:n], hi[:, sl, :, 0:n].bitcast(F32),
                              ALU.subtract).then_inc(s_lo, 1)

        def slots(eng, split, C, n, hooks, last=False):
            for s in range(n):
                g = s + LEAD
                if not (last and g >= n):
                    split(eng, C + g // 8, g % 8)
                for h in hooks.get(s, ()):
                    h()

        def mm_chunk(pe, C, par, Lh, Ll, hooks, s0=0, need=None, n=NC):
            if not (isinstance(C, int) and C < 2):
                pe.wait_ge(s_acc, C - 1)
            for j in range(8):
                sl = j % RING
                for (se, v) in (need or {}).get(j, ()):
                    pe.wait_ge(se, v)
                pe.wait_ge(s_lo, 8 * C + j + 1)
                for kk in range(2):
                    k = 2 * j + kk
                    for t in range(2):
                        o = acc[par][t][:, 0:n]
                        xh, xl = Lh[:, k, t * P:(t + 1) * P], Ll[:, k, t * P:(t + 1) * P]
                        wh, wl = hi[:, sl, kk, 0:n], lo[:, sl, kk, 0:n]
                        pe.matmul(o, xh, wh, start=(k == 0), stop=False)
                        pe.matmul(o, xh, wl, start=False, stop=False)
                        x = pe.matmul(o, xl, wh, start=False, stop=(k == KT - 1))
                x.then_inc(s_mm, 1)
                for h in hooks.get(s0 + j, ()):
                    h()

        def pe_event(pe, e, ready=()):
            if not (isinstance(e, int) and e == 0):
                pe.wait_ge(s_tra, 2 * e)
                pe.wait_ge(s_trd, e)
            for (se, v) in ready:
                pe.wait_ge(se, v)

        def pe_turn(pe, e, src, ready=(), banks=None, sm=None):
            if banks is None:
                pe_event(pe, e, ready)
            else:
                for (se, v) in ready:
                    pe.wait_ge(se, v)
            for b in range(2):
                for ct in (2 * b, 2 * b + 1):
                    for t in range(2):
                        x = pe.transpose((banks or TR)[b][:, (ct % 2) * S + t * P:(ct % 2) * S + (t + 1) * P],
                                         src[:, t, ct * P:(ct + 1) * P], identf[:, :])
                x.then_inc(sm or s_tr, 1)

        def act_split_t(act, e, Lh, k0, wc=None, banks=None, sm=None, done=None):
            for b in range(2):
                act.wait_ge(sm or s_tr, 2 * e + b + 1)
                for c in range(2):
                    ct = 2 * b + c
                    o = Lh[:, k0 + ct, :] if isinstance(k0, int) else Lh[:, ds(k0 + ct, 1), :]
                    src = (banks or TR)[b][:, c * S:(c + 1) * S]
                    if not isinstance(k0, int):
                        src = src.unsqueeze(1)
                    x = act.activation(o, src, ACT.Copy, scale=wc[:, ct:ct + 1] if wc is not None else 1.0)
                x.then_inc(done or s_tra, 1)

        def dve_split_t(dve, e, Lh, Ll, k0, wc=None, banks=None, sa=None, done=None):
            for b in range(2):
                dve.wait_ge(sa or s_tra, 2 * e + b + 1)
                for c in range(2):
                    ct = 2 * b + c
                    dyn = not isinstance(k0, int)
                    o = Ll[:, ds(k0 + ct, 1), :] if dyn else Ll[:, k0 + ct, :]
                    h = Lh[:, ds(k0 + ct, 1), :] if dyn else Lh[:, k0 + ct, :]
                    src = (banks or TR)[b][:, c * S:(c + 1) * S]
                    if dyn:
                        src = src.unsqueeze(1)
                    if wc is None:
                        x = dve.tensor_tensor(o, src, h.bitcast(F32), ALU.subtract)
                    else:
                        x = dve.scalar_tensor_tensor(o, src, wc[:, ct:ct + 1], h.bitcast(F32), ALU.mult, ALU.subtract)
            x.then_inc(done or s_trd, 1)


        XCT = sb("XCT", [P, 8, S])
        XC = XCT[:, 0:4, :]
        TH = XCT[:, 4:8, :]
        XP = XCT[:, :, :].rearrange("p a s -> p (a s)")[:, 0:CMP * NG * NCMP].rearrange(
            "p (i g j) -> p i g j", i=CMP, g=NG)
        early = BCT[:, :, :].rearrange("p a s -> p (a s)")
        used = [0]

        def view(size, pattern=None, **kw):
            v = early[:, used[0]:used[0] + size]
            used[0] += size
            assert used[0] <= KT * S
            return v.rearrange(pattern, **kw) if pattern else v

        NAT = view(4 * P, "p (n c) -> p n c", n=4)
        zz = view(P)
        KV = view(NG * S, "p (g s) -> p g s", g=NG)
        HT = view(NG * NCMP)
        HS = view(NG * NCMP)
        KCN = view(2 * HD, "p (n d) -> p n d", n=2)[0:NG * NCMP, :, :]
        W2 = view(2 * HD, "p (n d) -> p n d", n=2)
        ROWS = view(3 * SH, "p (n h) -> p n h", n=3)
        SM = view(2 * SMALL, "p (t n) -> p t n", t=2)
        TM = view(10 * SH, "p (n t h) -> p n t h", n=5, t=2)
        ANG = view(3 * SH, "p (n h) -> p n h", n=3)
        KK = view(3 * SH, "p (n h) -> p n h", n=3)
        RR = Y[:, 0, 0:6 * SH].rearrange("p (f n h) -> p f n h", f=2, n=3)

        def QT(r0, r1):
            t, b = r0 // 2, r0 % 2
            return GB[:, t, D - NC + b * S:D - NC + (b + r1 - r0) * S]

        def V_(t, b):
            return V3[:, 2 * t + b, :] if t + b < 2 else GA[:, 1, D - NC:D]

        VCB = GA[0:NCMP, 0, D - NC:D].rearrange("p (g d) -> p g d", g=NG)
        flat_y = Y[:, :, :].rearrange("p t n -> p (t n)")
        PTS = flat_y[:, 0:768].rearrange("p (n q) -> p n q", n=2)
        PTC = flat_y[0:NCMP, 768:1024].rearrange("p (n q) -> p n q", n=2)

        pre = ExitStack()
        TAB = sb("TAB", [P, 2, 3, P], c=pre)
        KT_ = sb("KT", [P, 2, NG, S], c=pre)
        V3 = sb("V", [P, 3, NC], c=pre)
        PB = sb("PB", [P, 768], c=pre)
        VSs = sb("VSs", [P, 2, 2, HD], c=pre)
        KCT = sb("KCT", [P, NG, NCMP], c=pre)
        VCs = sb("VCs", [NCMP, HD], c=pre)
        MX = sb("MX", [P, 6], c=pre)
        NM = sb("NM", [P, 6], c=pre)
        SUM = sb("SUM", [P, 6], c=pre)
        SCB = sb("SCB", [P, 2, NCMP], c=pre)
        EC = sb("EC", [P, 2, NCMP], c=pre)
        PC = sb("PC", [P, 2, NCMP], c=pre)
        CM1 = sb("CM1", [P, 2, NCMP], c=pre)
        CNEG = sb("CNEG", [P, 2, NCMP], c=pre)
        POSI = sb("POSI", [P, 3], I32, c=pre)
        POS = sb("POS", [P, 3], c=pre)
        pre.close()
        post = ExitStack()
        XTOK = sb("XTOK", [P, 2, NC], c=post)
        XDT = sb("XDT", [P, 2, NC], c=post)
        XDS = sb("XDS", [P, NC], c=post)
        BTg = sb("BTg", [P, S], c=post)
        CTg = sb("CTg", [P, S], c=post)
        dAg = sb("dAg", [P, 2, 8], c=post)
        NWs = sb("NWs", [P, 4], c=post)
        W = sb("W", [P, 4, NC], c=post)
        ZT = sb("ZT", [P, 2, NC], c=post)
        post.close()
        flat_th = TH.rearrange("p a s -> p (a s)")
        CBB = flat_th[:, 0:3 * P].rearrange("p (n l) -> p n l", n=3)
        ST = flat_th[:, NC:2 * NC]
        XD = XTOK
        ZR = XR
        block = ctx.enter_context(nc.Block())

        def heads4(x):
            return x.rearrange("p (h d) -> p h d", h=4)

        def heads8(x):
            return x.rearrange("p (h d) -> p h d", h=8)

        w1v = (GA, GB)
        x_rows = a["x"][0].rearrange("(t p) d -> p t d", p=P)
        out_rows = out[0].rearrange("(t p) d -> p t d", p=P)

        @block.sync
        def _(sp):
            for t in range(2):
                sp.dma_start(GA[:, t, :], x_rows[:, t, :]).then_inc(s_x, 16)
            w_na = a["w_proj_nsa"].rearrange("(k p) c -> p k c", p=P)
            w_ss = a["w_proj_ssm"].rearrange("(k p) c -> p k c", p=P)
            w_ou = a["w_out"].rearrange("(k p) c -> p k c", p=P)
            w_up = a["w_up"].rearrange("(k p) c -> p k c", p=P)
            w_dn = a["w_down"].rearrange("(k p) c -> p k c", p=P)
            load_chunk(sp, C_SMALL, w_in, 0, 0, extra=[(w_in, NG0, 0, 3 * NH), (w_in, DT0, 3 * NH, SH)])
            for C, c0 in ((C_KC, KC0), (C_VC, VC0), (C_KS, KS0), (C_VS, VS0), (C_KW, KW0), (C_VW, VW0)):
                load_chunk(sp, C, w_in, 0, c0)
            with sp.Fori(0, NG) as i:
                for k, c0 in enumerate((0, XBC0 + DI, GATE0, GATE0 + D)):
                    load_chunk(sp, C_AT + 4 * i + k, w_in, 0, c0 + NC * i)
            with sp.Fori(0, 2) as i:
                for k in range(2):
                    load_chunk(sp, C_PA + 2 * i + k, w_na, 0, 2 * NC * i + NC * k)
            load_chunk(sp, C_X0, w_in, 0, XBC0)
            load_chunk(sp, C_X0 + 1, w_in, 0, Z0)
            with sp.Fori(0, 4) as i:
                load_chunk(sp, C_L1 + 2 * i, w_in, 0, XBC0 + NC + NC * i)
                load_chunk(sp, C_L1 + 2 * i + 1, w_in, 0, Z0 + NC + NC * i)
            with sp.Fori(0, 2) as i:
                for k in range(2):
                    load_chunk(sp, C_PB1 + 2 * i + k, w_ss, 0, 2 * NC * i + NC * k)
            with sp.Fori(0, 3) as i:
                load_chunk(sp, C_L2 + 2 * i, w_in, 0, XBC0 + 5 * NC + NC * i)
                load_chunk(sp, C_L2 + 2 * i + 1, w_in, 0, Z0 + 5 * NC + NC * i)
            for n in range(4):
                load_chunk(sp, C_PB2 + n, w_ss, KT, NC * n)
            for n in range(4):
                load_chunk(sp, C_WO + n, w_ou, 0, NC * n)
            with sp.Fori(0, 4) as i:
                for k in range(4):
                    load_chunk(sp, C_MLP + 8 * i + k, w_up, 0, D * i + NC * k)
                for k in range(4):
                    load_chunk(sp, C_MLP + 8 * i + 4 + k, w_dn, KT * i, NC * k)
            for t in range(2):
                sp.wait_ge(s_fin, t + 1)
                sp.dma_start(out_rows[:, t, :], GB[:, t, :]).then_inc(s_out, 16)
            sp.wait_ge(s_out, 32)

        @block.gpsimd
        def _(pool):
            pool.memset(identf[:, :], 0.0)
            pool.memset(zz[:, :], 0.0)
            pool.memset(ones[:, :], 1.0)
            pool.memset(mhalf[:, :], -0.5)
            pool.memset(POSI[:, :], 0)
            pool.drain()
            pool.affine_select(identf[:, :], identf[:, :], [[-1, P]], ALU.not_equal, 1.0, base=0, channel_multiplier=1)
            pool.affine_select(tri[:, :], ones[:, :], [[1, P]], ALU.is_ge, 0.0, base=0, channel_multiplier=-1)
            pool.affine_select(maskq[:, :], zz[:, :], [[-1, P]], ALU.is_ge, NEG, base=0, channel_multiplier=1)
            pool.affine_select(maskt[:, :], zz[:, :], [[1, P]], ALU.is_ge, NEG, base=0, channel_multiplier=-1)
            cm = [[P, 2], [-STR, NCMP]]
            one30 = ones[:, 0:2 * NCMP].rearrange("p (t j) -> p t j", t=2)
            zero30 = zz[:, 0:2 * NCMP].rearrange("p (t j) -> p t j", t=2)
            pool.affine_select(CM1[:, :, :], one30, cm, ALU.is_ge, 0.0, base=1 - CMP, channel_multiplier=1)
            pool.affine_select(CNEG[:, :, :], zero30, cm, ALU.is_ge, NEG, base=1 - CMP, channel_multiplier=1)
            pool.drain().then_inc(s_const, 1)
            small = [
                (NAT[0:16, 0, :], a["norm_mix_w"].rearrange("(k p) -> k p", p=P)),
                (NAT[16:48, 0, :], a["ssm_norm_w"].rearrange("(k p) -> k p", p=P)),
                (NAT[48:64, 0, :], a["norm_mlp_w"].rearrange("(k p) -> k p", p=P)),
                (NAT[64:112, 0, :], a["conv_b"].rearrange("(k p) -> k p", p=P)),
                (NAT[0:96, 1, :], a["conv_w"].rearrange("i (k p) -> (i k) p", p=P)[0:96, :]),
                (NAT[0:96, 2, :], a["conv_w"].rearrange("i (k p) -> (i k) p", p=P)[96:192, :]),
                (NAT[0:32, 3, :], a["cmp_pos_k"]),
                (NAT[32:64, 3, :], a["cmp_pos_v"]),
                (ROWS[:, 0, :], a["dt_bias"].partition_broadcast(P)),
                (ROWS[:, 1, :], a["a_log"].partition_broadcast(P)),
                (ROWS[:, 2, :], a["inv_freq"].partition_broadcast(P)),
                (DBC[:, :], a["ssm_d"].partition_broadcast(P)),
                (POSI[:, 0:2], a["positions"][0].rearrange("(t p) -> p t", p=P)),
            ] + [(POSI[NCMP * g:NCMP * (g + 1), 2:3],
                  a["positions"][0][STR:S].rearrange("(j i) -> j i", i=STR)[:, STR - 1:STR]) for g in range(NG)]
            for o, i_ in small:
                pool.dma_start(o, i_, allow_slow_non_contiguous=True).then_inc(s_small, 16)
            assert len(small) == N_SMALL
            pool.wait_ge(s_v, 1)
            pool.tensor_tensor(RS[:, 0:2], VV[:, 0:2], mhalf[:, 0:2], ALU.pow).then_inc(s_pow, 1)
            pool.wait_ge(s_trd, 4)
            for n, w in enumerate(("cmp_k_w1", "cmp_v_w1")):
                pool.dma_start(w1v[n][:, :, :].rearrange("p t n -> p (t n)").rearrange("p (i h) -> p i h", i=CMP),
                               a[w].rearrange("(i d) h -> d i h", d=P)).then_inc(s_w12, 16)
            for n, w in enumerate(("cmp_k_w2", "cmp_v_w2")):
                pool.dma_start(W2[:, n, :], a[w]).then_inc(s_w12, 16)

            def stage_conv(tile):
                taps = COLS[:, CCW:CCW + 192].rearrange("p (i t) -> p i t", i=4)
                pool.tensor_copy(CWs[:, 0:4, :], taps[:, :, ds(tile, 4)]).then_inc(s_cw, 1)
                pool.tensor_copy(CWs[:, 4, :], COLS[:, ds(tile + CCB, 4)]).then_inc(s_cw, 1)

            pool.wait_ge(s_kcr, 2)
            pool.wait_ge(s_vcd, 1)
            pool.wait_ge(s_acc, C_AT)
            with pool.Fori(0, NG) as i:
                e = E_AT + PER_AT * i
                pool.wait_ge(s_tr, 2 * e)
                pool.wait_ge(s_tra, 2 * e)
                pool.wait_ge(s_trd, e)
                for kt in range(2):
                    for b in range(2):
                        pool.tensor_copy(VSs[:, kt, b, :], V_(kt, b)[:, ds(HD * i, HD)]).then_inc(s_stage, 1)
                pool.tensor_copy(VCs[:, :].unsqueeze(1), VCB[:, ds(i, 1), :]).then_inc(s_stage, 1)
                stage_conv(32 + 4 * i)

            def stage_scan(g):
                pool.wait_ge(s_e3d, g + 1)
                pool.tensor_copy(BTg[:, :].unsqueeze(1), BCT[:, ds(g, 1), :]).then_inc(s_pg, 1)
                pool.tensor_copy(CTg[:, :].unsqueeze(1), BCT[:, ds(g + 8, 1), :]).then_inc(s_pg, 1)
                pool.tensor_copy(dAg[:, :, :], DA[:, :, ds(8 * g, 8)]).then_inc(s_pg, 1)
                pool.tensor_copy(NWs[:, :], COLS[:, ds(4 * g + CSN, 4)]).then_inc(s_pg, 1)

            def skip_term(g, e):
                pool.wait_ge(s_trd, e + 1)
                for t in range(2):
                    pool.tensor_tensor(heads8(XD[:, t, :]), heads8(XTOK[:, t, :]),
                                       DBC[:, ds(8 * g, 8)].unsqueeze(2).broadcast_to([P, 8, SH]),
                                       ALU.mult).then_inc(s_xdd, 1)

            def rsqrt(n, o, i_):
                pool.wait_ge(s_v, n)
                pool.tensor_tensor(o, i_, mhalf[:, 0:2], ALU.pow).then_inc(s_pow, 1)

            pool.wait_ge(s_trd, E_X0)
            pool.wait_ge(s_tra, 2 * E_X0)
            stage_conv(0)
            skip_term(0, E_X0 + 1)

            def scan_iteration(i, t, e):
                stage_scan(t - 1)
                pool.wait_ge(s_trd, e)
                stage_conv(4 * t)
                rsqrt(1 + t, RS[:, 0:2], VV[:, 0:2])
                skip_term(t, e + 1)

            with pool.Fori(0, 4) as i:
                scan_iteration(i, 1 + i, E_L1 + 2 * i)
            with pool.Fori(0, 3) as i:
                scan_iteration(i, 5 + i, E_L2 + 2 * i)
            stage_scan(7)
            rsqrt(9, RS[:, 0:2], VV[:, 0:2])
            pool.wait_ge(s_pg, 32)
            for t in range(2):
                pool.dma_start(H[:, t, :], x_rows[:, t, :]).then_inc(s_hr, 16)
            pool.wait_ge(s_mg, 4)
            pool.dma_start(GA[:, 0, :], a["norm_final_w"].partition_broadcast(P)).then_inc(s_wf, 16)
            rsqrt(10, RS[:, 2:4], VV[:, 0:2])
            rsqrt(11, RS[:, 0:2], VV[:, 0:2])

        @block.tensor
        def _(pe):
            pe.wait_ge(s_const, 1)
            pe.wait_ge(s_small, 16 * N_SMALL)
            for n, (r, c) in enumerate(((112, 0), (96, 112), (96, 208), (64, 304))):
                x = pe.transpose(X6[:, c:c + r], NAT[0:r, n, :], identf[0:r, 0:r])
            x.then_inc(s_colp, 1)
            for n in range(4):
                pe_turn(pe, E_U + n, GB[:, :, NC * n:NC * (n + 1)], [(s_u, n + 1)])
            mm_chunk(pe, C_SMALL, 0, LAh, LAl, {}, n=SMALL, need={2 * n: [(s_trd, n + 1)] for n in range(4)})

            def cumsum():
                pe.wait_ge(s_dts, 2)
                da = DA[:, :, :].rearrange("p t h -> p (t h)")
                pe.wait_ge(s_colc, 1)
                pe.matmul(X6[:, 0:P], tri[:, :], da, start=True, stop=True)
                pe.matmul(X6[:, P:2 * P], ones[:, :], da, start=True, stop=True).then_inc(s_acs, 1)

            def compress(n):
                pe.wait_ge(s_xp, n + 1)
                pe.wait_ge(s_w12, 64)
                w = w1v[n][:, :, :].rearrange("p t n -> p (t n)")
                for i in range(CMP):
                    x = pe.matmul(X7[:, 0:NG * NCMP], w[:, HD * i:HD * (i + 1)],
                                  XP[:, i, :, :].rearrange("p g j -> p (g j)"), start=(i == 0), stop=(i == CMP - 1))
                x.then_inc(s_hid, 1)

            def compress_k2():
                pe.wait_ge(s_hs, 1)
                pe.wait_ge(s_dts, 3)
                pe.matmul(X6[0:NG * NCMP, 0:HD], HS[:, :], W2[:, 0, :], start=True, stop=True).then_inc(s_hid, 1)

            def compress_k3():
                pe.wait_ge(s_kcr, 1)
                n = NG * NCMP
                pe.transpose(X6[:, P:P + n], KCN[:, 0, :], identf[0:n, 0:n]).then_inc(s_hid, 1)

            def compress_v2():
                pe.wait_ge(s_hs, 2)
                pe.wait_ge(s_kcr, 2)
                for g in range(NG):
                    x = pe.matmul(X6[0:NCMP, HD * g:HD * (g + 1)], HS[:, NCMP * g:NCMP * (g + 1)], W2[:, 1, :],
                                  start=True, stop=True)
                x.then_inc(s_hid, 1)

            mm_chunk(pe, C_KC, 1, LAh, LAl, {5: [cumsum]})
            mm_chunk(pe, C_VC, 0, LAh, LAl, {2: [lambda: pe_turn(pe, E_KC, XR, [(s_acc, C_KC + 1)])],
                                             6: [lambda: compress(0)]})
            mm_chunk(pe, C_KS, 1, LAh, LAl, {0: [compress_k2],
                                             2: [lambda: pe_turn(pe, E_VC, XR, [(s_acc, C_VC + 1)])],
                                             4: [compress_k3], 6: [lambda: compress(1)]})
            mm_chunk(pe, C_VS, 0, LAh, LAl, {0: [compress_v2],
                                             2: [lambda: pe_turn(pe, E_KS, Y, [(s_rope, 1)])]})
            mm_chunk(pe, C_KW, 1, LAh, LAl, {})
            mm_chunk(pe, C_VW, 0, LAh, LAl, {2: [lambda: pe_turn(pe, E_KW, Y, [(s_rope, 2)])]})

            def scores(i, r, e):
                n = 4 * i + r
                pe.wait_ge(s_tra, 2 * e + 2)
                pe.wait_ge(s_trd, e + 1)
                pe.wait_ge(s_stage, 5 * i + 5)
                pe.wait_ge(s_ex, n + 1)
                q0, q1 = QT(r, r + 1)[:, 0:P], QT(r, r + 1)[:, P:S]
                for b in range(2):
                    pe.matmul(X6[:, b * S + P:b * S + S], identb[:, :], maskq[:, :], start=(b == 0), stop=False,
                              skip_group_check=True)
                for b in range(2):
                    pe.matmul(X6[:, b * S:(b + 1) * S], q1, KT_[:, b, ds(i, 1), :].rearrange("p o s -> p (o s)"), start=False, stop=(b == 1),
                              skip_group_check=True)
                pe.matmul(X7[:, 0:S].rearrange("p (b k) -> p b k", b=2), identb[:, :],
                          maskq[:, :].unsqueeze(1).broadcast_to([P, 2, P]), start=True, stop=False, skip_group_check=True)
                for b in range(2):
                    pe.matmul(X7[:, b * P:(b + 1) * P], q0, KT_[:, b, ds(i, 1), 0:P].rearrange("p o s -> p (o s)"), start=False, stop=False, skip_group_check=True)
                for t, q in enumerate((q0, q1)):
                    x = pe.matmul(X7[:, S + NCMP * t:S + NCMP * (t + 1)], q, KCT[:, ds(i, 1), :].rearrange("p o s -> p (o s)"), start=False, stop=(t == 1),
                                  skip_group_check=True)
                x.then_inc(s_sc, 1)

            def turn_probs(i, r, e):
                pe_event(pe, e, [(s_p, 4 * i + r + 1)])
                for b in range(2):
                    pe.transpose(TR[b][:, 0:P], PB[:, 512 + P * b:512 + P * (b + 1)], identf[:, :])
                    for k in range(2):
                        pe.transpose(TR[b][:, P * (k + 1):P * (k + 2)], PB[:, S * b + P * k:S * b + P * (k + 1)], identf[:, :])
                    pe.transpose(TR[b][0:NCMP, 384:512], PC[:, b, :], identf[:, :]).then_inc(s_tr, 1)

            def values(i, r, e):
                pe_event(pe, e)
                for b in range(2):
                    pe.matmul(TR[0][:, 0:S], VSs[:, 0, b, :], PTS[:, b, 0:S], start=(b == 0), stop=False,
                              skip_group_check=True)
                    x = pe.matmul(TR[0][:, P:S], VSs[:, 1, b, :], PTS[:, b, S:384], start=False, stop=False,
                                  skip_group_check=True)
                x.then_inc(s_tr, 1)
                pe.matmul(TR[0][:, 0:S], VCs[:, :], PTC[:, :, :].rearrange("p t q -> p (t q)"), start=False, stop=True,
                          skip_group_check=True).then_inc(s_tr, 1)

            with pe.Fori(0, NG) as i:
                C, e = C_AT + 4 * i, E_AT + PER_AT * i
                hooks = {SL_Q: [lambda: pe_turn(pe, e + EQ, Y, [(s_rope, i + 3)])],
                         SL_BC: [lambda: pe_turn(pe, e + EBC, XR, [(s_acc, C + 2)])]}
                for r in range(4):
                    hooks.setdefault(SL_PV[r], []).append(lambda r=r: values(i, r, e + EPV[r]))
                for r in range(4):
                    hooks.setdefault(SL_PT[r], []).append(lambda r=r: turn_probs(i, r, e + EPT[r]))
                for r in range(4):
                    hooks.setdefault(SL_S[r], []).append(lambda r=r: scores(i, r, e))
                for k in range(4):
                    mm_chunk(pe, C + k, (C_AT + k) % 2, LAh, LAl,
                             {s - 8 * k: v for s, v in hooks.items() if s // 8 == k})
            with pe.Fori(0, 2) as i:
                for k in range(2):
                    mm_chunk(pe, C_PA + 2 * i + k, (C_PA + k) % 2, LBh, LBl, {}, need={7: [(s_trd, E_X0)]})

            def scan_cb(g):
                pe.wait_ge(s_pg, 4 * g + 4)
                pe.wait_ge(s_e3d, g + 1)
                pe.transpose(X7[:, 2 * P:3 * P], BTg[:, 0:P], identf[:, :])
                for c in range(2):
                    x = pe.matmul(X7[:, c * P:(c + 1) * P], BTg[:, c * P:(c + 1) * P], CTg[:, c * P:(c + 1) * P],
                                  start=True, stop=True)
                x.then_inc(s_cb, 1)

            def scan_decay(g, b):
                c, hb = b // 2, b % 2
                if b:
                    pe.wait_ge(s_sub, 4 * g + b)
                pe.matmul(X6[:, :].rearrange("p (h l) -> p h l", h=4), identb[:, :],
                          maskt[:, :].unsqueeze(1).broadcast_to([P, 4, P]), start=True, stop=False, skip_group_check=True)
                for h in range(4):
                    x = pe.matmul(X6[:, h * P:(h + 1) * P], dAg[:, c, 4 * hb + h:4 * hb + h + 1].broadcast_to([P, P]),
                                  tri[:, :], start=False, stop=(h == 3), skip_group_check=True)
                x.then_inc(s_dk, 1)

            def scan_state(g):
                pe.wait_ge(s_cbc, g + 1)
                pe.wait_ge(s_xd, g + 1)
                pe.matmul(X7[:, :], CBB[:, 2, :], XDS[:, :], start=True, stop=True).then_inc(s_st, 1)

            def scan_y(c):
                for h in range(8):
                    x = pe.matmul(X7[:, h * SH:(h + 1) * SH], W[:, 2 * c + h // 4, (h % 4) * P:(h % 4 + 1) * P],
                                  XDT[:, c, h * SH:(h + 1) * SH], start=True, stop=True)
                return x

            def scan_y0(g):
                pe.wait_ge(s_stc, g + 1)
                pe.wait_ge(s_w, 4 * g + 2)
                scan_y(0).then_inc(s_y0, 1)

            def scan_y1(g):
                pe.wait_ge(s_y0d, g + 1)
                pe.wait_ge(s_w, 4 * g + 4)
                pe.matmul(X6[:, :], CTg[:, P:S], ST[:, :], start=True, stop=True)
                scan_y(1).then_inc(s_ey, 1)

            def scan_turn_y(g):
                pe_turn(pe, None, Y, [(s_yn, g + 1)], banks=(X6, X7), sm=s_e3)

            def scan_hooks(g):
                return {0: [lambda: scan_cb(g), lambda: scan_decay(g, 0)], 2: [lambda: scan_decay(g, 1)],
                        3: [lambda: scan_state(g)], 4: [lambda: scan_decay(g, 2)], 5: [lambda: scan_y0(g)],
                        6: [lambda: scan_decay(g, 3)], 8: [lambda: scan_y1(g)], 12: [lambda: scan_turn_y(g)]}

            def turn_back(e, m):
                pe_event(pe, e, [(s_xs, m + 2)])
                for t in range(2):
                    for ct in range(4):
                        x = pe.transpose(TR[t][:, ct * P:(ct + 1) * P], XC[:, ct, t * P:(t + 1) * P], identf[:, :])
                    x.then_inc(s_tr, 1)

            def scan_iteration(C, par, e, m, g=None):
                hooks = scan_hooks(g) if g is not None else {}
                hooks[9] = [lambda: pe_turn(pe, e, XR, [(s_acc, C + 1)])]
                hooks[13] = [lambda: turn_back(e + 1, m)]
                for k in range(2):
                    mm_chunk(pe, C + k, (par + k) % 2, LAh, LAl, {s - 8 * k: v for s, v in hooks.items() if s // 8 == k})

            scan_iteration(C_X0, C_X0 % 2, E_X0, 4)
            with pe.Fori(0, 4) as i:
                scan_iteration(C_L1 + 2 * i, C_L1 % 2, E_L1 + 2 * i, 5 + i, i)
            with pe.Fori(0, 2) as i:
                for k in range(2):
                    mm_chunk(pe, C_PB1 + 2 * i + k, (C_PB1 + k) % 2, LBh, LBl, {}, need={0: [(s_e3d, 5)]})
            with pe.Fori(0, 3) as i:
                scan_iteration(C_L2 + 2 * i, C_L2 % 2, E_L2 + 2 * i, 9 + i, i + 4)
            for s, v in scan_hooks(7).items():
                for h in v:
                    h()
            for n in range(4):
                hooks = {2: [lambda: pe_turn(pe, E_PB2 + n - 1, Y, [(s_mg, n)])]} if n else {}
                mm_chunk(pe, C_PB2 + n, (C_PB2 + n) % 2, LBh, LBl, hooks, need={6: [(s_e3d, 9)]})
            for n in range(4):
                hooks = ({2: [lambda: pe_turn(pe, E_WO + n - 1, H[:, :, NC * (n - 1):NC * n], [(s_acc, C_WO + n)])]} if n
                         else {2: [lambda: pe_turn(pe, E_PB2 + 3, Y, [(s_mg, 4)])]})
                mm_chunk(pe, C_WO + n, (C_WO + n) % 2, LAh, LAl, hooks, need={6: [(s_trd, E_PB2 + 4)]})
            pe_turn(pe, E_WO + 3, H[:, :, 3 * NC:4 * NC], [(s_acc, C_WO + 4)])
            with pe.Fori(0, 4) as i:
                C, e = C_MLP + 8 * i, E_MLP + 4 * i
                for k in range(4):
                    hooks = {2: [lambda: pe_turn(pe, e + k - 1, Y, [(s_ff, 4 * i + k)])]} if k else {}
                    mm_chunk(pe, C + k, (C_MLP + k) % 2, LBh, LBl, hooks, need={6: [(s_trd, E_MLP)]})
                for k in range(4):
                    hooks = {} if k else {2: [lambda: pe_turn(pe, e + 3, Y, [(s_ff, 4 * i + 4)])]}
                    mm_chunk(pe, C + 4 + k, (C_MLP + k) % 2, LAh, LAl, hooks, need={6: [(s_trd, e + 4)]})

        @block.scalar
        def _(act):
            def take(C, par, o, n=NC, func=ACT.Copy, scale=1.0):
                act.wait_ge(s_mm, 8 * C + 8)
                act.activation(o, acc[par][0][:, 0:n], func, scale=scale).then_inc(s_xa, 1)

            def copy_t(e, o):
                act.wait_ge(s_tr, 2 * e + 1)
                act.activation(o, TR[0][:, :].rearrange("p (a s) -> p a s", a=2), ACT.Copy).then_inc(s_tra, 2)

            for t in range(2):
                act.wait_ge(s_x, 32)
                act.activation(GB[:, t, :], GA[:, t, :], ACT.Square, accum_out=SS[:, t:t + 1]).then_inc(s_ss, 1)
            for j in range(LEAD):
                split_hi(act, C_SMALL, j)
            act.wait_ge(s_colc, 1)
            for n in range(4):
                act_split_t(act, E_U + n, LAh, 4 * n, COLS[:, CN1 + 4 * n:CN1 + 4 * n + 4])
            act.wait_ge(s_ang, 1)
            for half, sc in ((0, -1.0), (1, 1.0)):
                act.activation(TAB[:, 0, :, 64 * half:64 * half + 64], RR[:, 0, :, :], ACT.Sin, scale=sc).then_inc(s_sin, 1)
                act.activation(TAB[:, 1, :, 64 * half:64 * half + 64], RR[:, 1, :, :], ACT.Sin).then_inc(s_sin, 1)

            def gates_dt():
                take(C_SMALL, 0, SM[:, 0, :], SMALL)
                act.wait_ge(s_acc, 1)
                act.activation(SM[:, :, 0:3 * NH], SM[:, :, 0:3 * NH], ACT.Tanh, scale=0.5).then_inc(s_dta, 1)
                act.wait_ge(s_small, 16 * N_SMALL)
                act.activation(ROWS[:, 1, :], ROWS[:, 1, :], ACT.Exp).then_inc(s_dta, 1)
                act.wait_ge(s_dts, 1)
                act.activation(TM[:, 2, :, :], TM[:, 1, :, :], ACT.Exp, scale=-1.0).then_inc(s_dta, 1)
                act.drain()
                act.activation(TM[:, 3, :, :], TM[:, 2, :, :], ACT.Ln, bias=1.0).then_inc(s_dta, 1)

            def decay_ends():
                act.wait_ge(s_dts, 3)
                act.activation(DST[:, :], DST[:, :], ACT.Exp).then_inc(s_dta, 1)
                act.activation(EA1[:, :], ACS[:, 1, :], ACT.Exp).then_inc(s_dta, 1)

            def hidden(n, cnt):
                act.wait_ge(s_hid, cnt)
                act.activation(HT[:, :], X7[:, 0:NG * NCMP], ACT.Tanh, scale=0.5).then_inc(s_hta, 1)

            slots(act, split_hi, C_SMALL, 8, {7: [gates_dt]})
            slots(act, split_hi, C_KC, 8, {6: [decay_ends], 7: [lambda: take(C_KC, 1, XR[:, 0, :])]})
            slots(act, split_hi, C_VC, 8, {2: [lambda: copy_t(E_KC, KV[:, 0:2, :])], 6: [lambda: hidden(0, 1)],
                                           7: [lambda: take(C_VC, 0, XR[:, 0, :])]})
            slots(act, split_hi, C_KS, 8, {2: [lambda: copy_t(E_VC, KV[:, 0:2, :])], 6: [lambda: hidden(1, 4)],
                                           7: [lambda: take(C_KS, 1, XR[:, 0, :])]})
            slots(act, split_hi, C_VS, 8, {2: [lambda: copy_t(E_KS, KT_[:, 0, 0:2, :])],
                                           7: [lambda: take(C_VS, 0, V_(0, 0))]})
            slots(act, split_hi, C_KW, 8, {7: [lambda: take(C_KW, 1, XR[:, 0, :])]})
            slots(act, split_hi, C_VW, 8, {2: [lambda: copy_t(E_KW, KT_[:, 1, 0:2, :])],
                                           7: [lambda: take(C_VW, 0, V_(0, 1))]})

            def exps(n):
                act.wait_ge(s_nm, n + 1)
                for k in range(4):
                    b = k % 2
                    o = PB[:, S * b:S * (b + 1)] if k < 2 else PB[:, 512 + P * b:512 + P * (b + 1)]
                    src = X6[:, S * b:S * (b + 1)] if k < 2 else X7[:, P * b:P * (b + 1)]
                    act.activation(o, src, ACT.Exp, scale=SCALE, bias=NM[:, k:k + 1], accum_out=SUM[:, k:k + 1])
                act.activation(EC[:, :, :], SCB[:, :, :], ACT.Exp).then_inc(s_ex, 1)

            def copy_probs(e):
                act.wait_ge(s_tr, 2 * e + 1)
                act.activation(PTS[:, 0, :], TR[0][:, 0:384], ACT.Copy).then_inc(s_tra, 1)
                act.activation(PTC[:, 0, :], TR[0][0:NCMP, 384:512], ACT.Copy).then_inc(s_tra, 1)

            def head_out(h, e):
                act.wait_ge(s_tr, 2 * e + 2)
                act.activation(LBh[:, ds(h, 1), :], TR[0][:, 0:S].unsqueeze(1), ACT.Copy).then_inc(s_tra, 2)

            def conv(e, m):
                act.wait_ge(s_cw, 2 * m + 2)
                act.wait_ge(s_xs, m + 1)
                for b in range(2):
                    act.wait_ge(s_tr, 2 * e + b + 1)
                    for c in range(2):
                        ct = 2 * b + c
                        x = act.activation(XC[:, ct, :], TR[b][:, c * S:(c + 1) * S], ACT.Identity,
                                           scale=CWs[:, 3, ct:ct + 1], bias=CWs[:, 4, ct:ct + 1])
                    x.then_inc(s_tra, 1)

            def conv_tanh(e, m):
                act.wait_ge(s_trd, e + 1)
                act.activation(TH[:, :, :], XC[:, :, :], ACT.Tanh).then_inc(s_ct, 1)

            def gate(C, par, G, c0):
                take(C, par, G[:, 0, ds(c0, NC)], func=ACT.Tanh, scale=0.5)
                act.wait_ge(s_acc, C + 1)
                act.activation(G[:, 1, ds(c0, NC)], G[:, 1, ds(c0, NC)], ACT.Tanh, scale=0.5).then_inc(s_gt, 1)

            act.drain().then_inc(s_ex, 1)
            with act.Fori(0, NG) as i:
                C, e = C_AT + 4 * i, E_AT + PER_AT * i
                hk = {7: [lambda: take(C, C_AT % 2, XR[:, 0, :])],
                      SL_Q: [lambda: copy_t(e + EQ, QT(0, 2).rearrange("p (a s) -> p a s", a=2))],
                      15: [lambda: take(C + 1, (C_AT + 1) % 2, XR[:, 0, :])],
                      SL_BC: [lambda: conv(e + EBC, i)],
                      SL_BC + 2: [lambda: conv_tanh(e + EBC, i)],
                      23: [lambda: gate(C + 2, C_AT % 2, GA, NC * i)],
                      31: [lambda: gate(C + 3, (C_AT + 1) % 2, GB, NC * i)]}
                for r in range(4):
                    hk.setdefault(SL_PV[r], []).append(lambda r=r: head_out(4 * i + r, e + EPV[r]))
                for r in range(4):
                    hk.setdefault(SL_PT[r], []).append(lambda r=r: copy_probs(e + EPT[r]))
                for r in range(4):
                    hk.setdefault(SL_S[r], []).append(lambda r=r: exps(4 * i + r))
                slots(act, split_hi, C, 32, hk)
            with act.Fori(0, 2) as i:
                slots(act, split_hi, C_PA + 2 * i, 16, {})

            def take_z(C, par, t):
                take(C, par, ZR[:, 0, :])
                act.wait_ge(s_acc, C + 1)
                act.activation(ZT[:, :, :], ZR[:, :, :], ACT.Tanh, scale=0.5).then_inc(s_zt, 1)

            def token_rows(e):
                for t in range(2):
                    act.wait_ge(s_tr, 2 * e + t + 1)
                    act.activation(XTOK[:, t, :], TR[t][:, :], ACT.Copy).then_inc(s_tra, 1)

            def scan_exp(g, b):
                act.wait_ge(s_sub, 4 * g + b + 1)
                act.activation(W[:, b, :], W[:, b, :], ACT.Exp).then_inc(s_dx, 1)

            def scan_state(g):
                act.wait_ge(s_st, g + 1)
                act.activation(ST[:, :], X7[:, :], ACT.Copy).then_inc(s_stc, 1)

            def scan_squares(g):
                act.wait_ge(s_yg, g + 1)
                for t in range(2):
                    act.activation(W[:, t, :], Y[:, t, :], ACT.Square, accum_out=SS[:, t:t + 1]).then_inc(s_ss, 1)

            def scan_hooks(g, k0):
                return {0: [lambda: scan_exp(g, 0)], 2: [lambda: scan_exp(g, 1)], 3: [lambda: scan_state(g)],
                        4: [lambda: scan_exp(g, 2)], 6: [lambda: scan_exp(g, 3)], 9: [lambda: scan_squares(g)],
                        12: [lambda: act_split_t(act, g, LBh, k0, NWs, banks=(X6, X7), sm=s_e3, done=s_e3a)]}

            def scan_iteration(C, par, e, m, g=None, k0=None):
                hk = scan_hooks(g, k0) if g is not None else {}
                hk[7] = [lambda: take(C, par, XR[:, 0, :])]
                hk[9] = hk.get(9, []) + [lambda: conv(e, m)]
                hk[11] = [lambda: conv_tanh(e, m)]
                hk[13] = [lambda: token_rows(e + 1)]
                hk[15] = [lambda: take_z(C + 1, (par + 1) % 2, m)]
                slots(act, split_hi, C, 16, hk)

            scan_iteration(C_X0, C_X0 % 2, E_X0, 4)
            with act.Fori(0, 4) as i:
                scan_iteration(C_L1 + 2 * i, C_L1 % 2, E_L1 + 2 * i, 5 + i, i, 4 * i)
            with act.Fori(0, 2) as i:
                slots(act, split_hi, C_PB1 + 2 * i, 16, {})
            with act.Fori(0, 3) as i:
                scan_iteration(C_L2 + 2 * i, C_L2 % 2, E_L2 + 2 * i, 9 + i, i + 4, 4 * i)
            for s, v in scan_hooks(7, 12).items():
                for h in v:
                    h()
            for n in range(4):
                slots(act, split_hi, C_PB2 + n, 8, {2: [lambda: act_split_t(act, E_PB2 + n - 1, LAh, 4 * n - 4)]} if n else {})

            def residual_squares(n):
                act.wait_ge(s_acc, C_WO + n + 1)
                for t in range(2):
                    act.activation(XC[:, 2 * t:2 * t + 2, :].rearrange("p a s -> p (a s)"), H[:, t, NC * n:NC * (n + 1)],
                                   ACT.Square, accum_out=SS2[:, t, n:n + 1]).then_inc(s_ss, 1)

            for n in range(4):
                w = COLS[:, CN2 + 4 * n - 4:CN2 + 4 * n]
                slots(act, split_hi, C_WO + n, 8,
                      {2: [lambda: act_split_t(act, E_WO + n - 1, LBh, 4 * n - 4, w) if n else
                           act_split_t(act, E_PB2 + 3, LAh, 12)], 7: [lambda: residual_squares(n)]})
            act_split_t(act, E_WO + 3, LBh, 12, COLS[:, CN2 + 12:CN2 + 16])
            act.wait_ge(s_pow, 10)

            def mlp(i, last=False):
                C, e = C_MLP + 8 * i, E_MLP + 4 * i
                hk = {}
                for k in range(4):
                    hk[8 * k + 7] = [lambda k=k: take(C + k, (C_MLP + k) % 2, XR[:, 0, :], func=ACT.Relu, scale=RS[:, 2:3])]
                    hk[8 * k + 10] = [lambda k=k: act_split_t(act, e + k, LAh, 4 * k)]
                slots(act, split_hi, C, 64, hk, last)

            with act.Fori(0, 3) as i:
                mlp(i)
            mlp(3, last=True)
            act.wait_ge(s_acc, C_END)
            for t in range(2):
                act.activation(LAl[:, 8 * t:8 * t + 8, :].rearrange("p a s -> p (a s)"), H[:, t, :], ACT.Square,
                               accum_out=SS[:, t:t + 1]).then_inc(s_ss, 1)

        @block.vector
        def _(dve):
            def take(C, par, o, xa, n=NC):
                dve.wait_ge(s_xa, xa)
                dve.tensor_copy(o, acc[par][1][:, 0:n]).then_inc(s_acc, 1)

            def copy_t(e, o):
                dve.wait_ge(s_tr, 2 * e + 2)
                dve.tensor_copy(o, TR[1][:, :].rearrange("p (a s) -> p a s", a=2)).then_inc(s_trd, 1)

            def rope():
                def hv(x):
                    return x.rearrange("p t (h d) -> p t h d", h=4)
                T2 = XC[:, :, :].rearrange("p a s -> p (a s)").rearrange("p (t n) -> p t n", t=2)
                cos = TAB[:, 1, 0:2, :].unsqueeze(2).broadcast_to([P, 2, 4, P])
                dve.tensor_tensor(hv(Y[:, :, :]), hv(XR[:, :, :]), cos, ALU.mult)
                for o, i_ in ((0, 64), (64, 0)):
                    sin = TAB[:, 0, 0:2, o:o + 64].unsqueeze(2).broadcast_to([P, 2, 4, 64])
                    dve.tensor_tensor(hv(T2)[:, :, :, o:o + 64], hv(XR[:, :, :])[:, :, :, i_:i_ + 64], sin, ALU.mult)
                dve.drain()
                dve.tensor_tensor(Y[:, :, :], Y[:, :, :], T2, ALU.add).then_inc(s_rope, 1)

            dve.wait_ge(s_const, 1)
            dve.tensor_copy(identb[:, :], identf[:, :]).then_inc(s_cdve, 1)
            dve.wait_ge(s_ss, 2)
            dve.tensor_scalar(VV[:, 0:2], SS[:, 0:2], 1.0 / D, EPS, ALU.mult, ALU.add).then_inc(s_v, 1)
            dve.wait_ge(s_pow, 1)
            for n in range(4):
                for t in range(2):
                    x = dve.tensor_scalar(GB[:, t, NC * n:NC * (n + 1)], GA[:, t, NC * n:NC * (n + 1)], RS[:, t:t + 1], None,
                                          ALU.mult)
                x.then_inc(s_u, 1)
            for j in range(LEAD):
                split_lo(dve, C_SMALL, j)
            dve.wait_ge(s_colp, 1)
            dve.tensor_copy(COLS[:, 0:CCB], X6[:, 0:CCB])
            dve.tensor_copy(COLS[:, CPK:CPK + 64], X6[:, CPK:CPK + 64])
            dve.tensor_scalar(COLS[:, CCB:CPK], X6[:, CCB:CPK], 0.5, None, ALU.mult)
            dve.drain().then_inc(s_colc, 1)
            for n in range(4):
                dve_split_t(dve, E_U + n, LAh, LAl, 4 * n, COLS[:, CN1 + 4 * n:CN1 + 4 * n + 4])

            dve.wait_ge(s_small, 16 * N_SMALL)
            dve.tensor_copy(POS[:, :], POSI[:, :])
            dve.drain()
            dve.tensor_tensor(ANG[:, :, :], ROWS[:, 2, :].unsqueeze(1).broadcast_to([P, 3, SH]),
                              POS[:, :].unsqueeze(2).broadcast_to([P, 3, SH]), ALU.mult)
            two_pi = 2.0 * np.pi
            c1 = 6.28125
            c2 = 1.93500518798828125e-3
            c3 = two_pi - c1 - c2
            lim = 3.1415925
            for f in range(2):
                steps = [(KK, ANG, 1.0 / two_pi, 0.25 * f), (KK, KK, 1.0, 12582912.0), (KK, KK, 1.0, -12582912.0)]
                for o, i_, m, ad in steps:
                    dve.drain()
                    dve.tensor_scalar(o[:, :, :], i_[:, :, :], m, ad, ALU.mult, ALU.add)
                r = RR[:, f, :, :]
                for prev, c in ((ANG[:, :, :], c1), (r, c2), (r, c3)):
                    dve.drain()
                    dve.scalar_tensor_tensor(r, KK[:, :, :], -c, prev, ALU.mult, ALU.add)
                dve.drain()
                dve.tensor_scalar(r, r, 0.5 * np.pi * f, None, ALU.add)
                dve.drain()
                dve.tensor_scalar(r, r, lim, -lim, ALU.min, ALU.max)
            dve.drain().then_inc(s_ang, 1)

            def gates_dt():
                take(C_SMALL, 0, SM[:, 1, :], 1, SMALL)
                dve.drain()
                raw_dt = SM[:, :, 3 * NH:SMALL]
                dve.tensor_tensor(TM[:, 0, :, :], raw_dt, ROWS[:, 0, :].unsqueeze(1).broadcast_to([P, 2, SH]), ALU.add)
                dve.drain()
                dve.tensor_scalar(TM[:, 1, :, :], TM[:, 0, :, :], -1.0, None, ALU.mult)
                dve.drain()
                dve.tensor_tensor(TM[:, 1, :, :], TM[:, 0, :, :], TM[:, 1, :, :], ALU.max).then_inc(s_dts, 1)
                dve.wait_ge(s_dta, 1)
                g = SM[:, :, 0:3 * NH].rearrange("p t (h b) -> p t h b", b=3)
                for o, i_ in ((GR[:, :, 0:2], g[:, 1, :, 1:3]), (GR[:, :, 2:4], g[:, 0, :, 1:3]),
                              (GR[:, :, 4:5], g[:, 0, :, 0:1]), (GR[:, :, 5:6], g[:, 1, :, 0:1])):
                    dve.tensor_scalar(o, i_, 0.5, 0.5, ALU.mult, ALU.add)
                dve.wait_ge(s_dta, 4)
                x0, d, e, ln, m = (TM[:, k, :, :] for k in range(5))
                dve.tensor_scalar(d, e, 1.0, None, ALU.add)
                dve.drain()
                dve.tensor_scalar(d, d, -1.0, None, ALU.add)
                dve.drain()
                dve.tensor_scalar(m, d, 0.0, None, ALU.is_equal)
                dve.drain()
                dve.tensor_tensor(d, d, m, ALU.add)
                dve.tensor_tensor(ln, ln, m, ALU.add)
                dve.drain()
                dve.reciprocal(d, d)
                dve.drain()
                dve.tensor_tensor(ln, ln, d, ALU.mult)
                dve.drain()
                dve.tensor_tensor(ln, ln, e, ALU.mult)
                dve.drain()
                dve.scalar_tensor_tensor(DT[:, :, :], x0, 0.0, ln, ALU.max, ALU.add)
                dve.drain()
                dve.scalar_tensor_tensor(DA[:, :, :], DT[:, :, :], -1.0, ROWS[:, 1, :].unsqueeze(1).broadcast_to([P, 2, SH]),
                                         ALU.mult, ALU.mult).then_inc(s_dts, 1)

            def cumsums():
                dve.wait_ge(s_acs, 1)
                dve.tensor_copy(ACS[:, :, :].rearrange("p t h -> p (t h)"), X6[:, 0:P])
                dve.drain()
                dve.tensor_tensor(DST[:, :], X6[:, P:P + SH], ACS[:, 0, :], ALU.subtract).then_inc(s_dts, 1)

            def blocks(n, e, c):
                copy_t(e, KV[:, 2:4, :])
                dve.wait_ge(s_tra, 2 * e + 2)
                dve.drain()
                q = KV[:, :, :].rearrange("p g (j i) -> p g j i", i=STR)
                for h in range(2):
                    x = dve.tensor_tensor(XP[:, STR * h:STR * (h + 1), :, :].rearrange("p i g j -> p g j i"), q[:, :, h:h + NCMP, :],
                                          COLS[:, c + STR * h:c + STR * (h + 1)].unsqueeze(1).unsqueeze(1).broadcast_to([P, NG, NCMP, STR]),
                                          ALU.add)
                dve.drain().then_inc(s_xp, 1)

            def hidden(n):
                dve.wait_ge(s_hta, n + 1)
                dve.scalar_tensor_tensor(HS[:, :], HT[:, :], 1.0, X7[:, 0:NG * NCMP], ALU.add, ALU.mult).then_inc(s_hs, 1)

            def key_rope():
                n = NG * NCMP
                dve.wait_ge(s_hid, 2)
                dve.tensor_scalar(KCN[:, 0, :], X6[0:n, 0:HD], 0.5, None, ALU.mult)
                dve.drain()
                dve.tensor_tensor(KCN[:, 1, 0:64], KCN[:, 0, 64:128], TAB[0:n, 0, 2, 0:64], ALU.mult)
                dve.tensor_tensor(KCN[:, 1, 64:128], KCN[:, 0, 0:64], TAB[0:n, 0, 2, 64:128], ALU.mult)
                dve.drain()
                dve.tensor_tensor(KCN[:, 0, :], KCN[:, 0, :], TAB[0:n, 1, 2, :], ALU.mult)
                dve.drain()
                dve.tensor_tensor(KCN[:, 0, :], KCN[:, 0, :], KCN[:, 1, :], ALU.add).then_inc(s_kcr, 1)

            def key_copy():
                dve.wait_ge(s_hid, 3)
                dve.tensor_copy(KCT[:, :, :].rearrange("p g j -> p (g j)"), X6[:, P:P + NG * NCMP]).then_inc(s_kcr, 1)

            def value_copy():
                dve.wait_ge(s_hid, 5)
                dve.tensor_scalar(VCB[:, :, :].rearrange("p g d -> p (g d)"), X6[0:NCMP, :], 0.5, None, ALU.mult).then_inc(s_vcd, 1)

            def take_rope(C, par, xa):
                take(C, par, XR[:, 1, :], xa)
                dve.drain()
                rope()

            slots(dve, split_lo, C_SMALL, 8, {7: [gates_dt]})
            slots(dve, split_lo, C_KC, 8, {5: [cumsums], 7: [lambda: take(C_KC, 1, XR[:, 1, :], C_KC + 1)]})
            slots(dve, split_lo, C_VC, 8, {2: [lambda: blocks(0, E_KC, CPK)], 6: [lambda: hidden(0)],
                                           7: [lambda: take(C_VC, 0, XR[:, 1, :], C_VC + 1)]})
            dve.wait_ge(s_sin, 4)
            slots(dve, split_lo, C_KS, 8, {1: [key_rope], 2: [lambda: blocks(1, E_VC, CPV)], 5: [key_copy],
                                           6: [lambda: hidden(1)], 7: [lambda: take_rope(C_KS, 1, C_KS + 1)]})
            slots(dve, split_lo, C_VS, 8, {1: [value_copy], 2: [lambda: copy_t(E_KS, KT_[:, 0, 2:4, :])],
                                           7: [lambda: take(C_VS, 0, V_(1, 0), C_VS + 1)]})
            slots(dve, split_lo, C_KW, 8, {7: [lambda: take_rope(C_KW, 1, C_KW + 1)]})
            slots(dve, split_lo, C_VW, 8, {2: [lambda: copy_t(E_KW, KT_[:, 1, 2:4, :])],
                                           7: [lambda: take(C_VW, 0, V_(1, 1), C_VW + 1)]})

            def maxima(n):
                dve.wait_ge(s_sc, n + 1)
                dve.tensor_reduce(MX[:, 0:2], X6[:, :].rearrange("p (b k) -> p b k", b=2), AX.X, ALU.max)
                dve.tensor_reduce(MX[:, 2:4], X7[:, 0:S].rearrange("p (b k) -> p b k", b=2), AX.X, ALU.max)
                dve.tensor_tensor(SCB[:, :, :], X7[:, S:S + 2 * NCMP].rearrange("p (t j) -> p t j", t=2), CNEG[:, :, :], ALU.add)
                dve.drain()
                dve.tensor_reduce(MX[:, 4:6], SCB[:, :, :], AX.X, ALU.max)
                dve.drain()
                dve.tensor_scalar(NM[:, :], MX[:, :], -SCALE, None, ALU.mult)
                dve.drain()
                dve.scalar_tensor_tensor(SCB[:, :, :], SCB[:, :, :], SCALE, NM[:, 4:6].unsqueeze(2).broadcast_to([P, 2, NCMP]),
                                         ALU.mult, ALU.add).then_inc(s_nm, 1)

            def scale_probs(n):
                dve.wait_ge(s_ex, n + 2)
                dve.tensor_tensor(EC[:, :, :], EC[:, :, :], CM1[:, :, :], ALU.mult)
                dve.drain()
                dve.tensor_reduce(SUM[:, 4:6], EC[:, :, :], AX.X, ALU.add)
                dve.drain()
                dve.tensor_scalar(SUM[:, :], SUM[:, :], TINY, None, ALU.max)
                dve.drain()
                dve.reciprocal(SUM[:, :], SUM[:, :])
                dve.drain()
                dve.tensor_tensor(SUM[:, :].unsqueeze(1), SUM[:, :].unsqueeze(1), GR[:, ds(n, 1), :], ALU.mult)
                dve.drain()
                for k in range(4):
                    b = k % 2
                    v = PB[:, S * b:S * (b + 1)] if k < 2 else PB[:, 512 + P * b:512 + P * (b + 1)]
                    dve.tensor_scalar(v, v, SUM[:, k:k + 1], None, ALU.mult)
                dve.tensor_tensor(PC[:, :, :], EC[:, :, :], SUM[:, 4:6].unsqueeze(2).broadcast_to([P, 2, NCMP]), ALU.mult)
                dve.drain().then_inc(s_p, 1)

            def copy_probs(e):
                dve.wait_ge(s_tr, 2 * e + 2)
                dve.tensor_copy(PTS[:, 1, :], TR[1][:, 0:384])
                dve.tensor_copy(PTC[:, 1, :], TR[1][0:NCMP, 384:512])
                dve.drain().then_inc(s_trd, 1)

            def head_out(h, e):
                dve.wait_ge(s_tra, 2 * e + 2)
                dve.tensor_tensor(LBl[:, ds(h, 1), :], TR[0][:, 0:S].unsqueeze(1), LBh[:, ds(h, 1), :].bitcast(F32),
                                  ALU.subtract).then_inc(s_trd, 1)

            def conv(e):
                for b in range(2):
                    dve.wait_ge(s_tra, 2 * e + b + 1)
                    for k in (1, 2, 3):
                        for c in range(2):
                            ct = 2 * b + c
                            x = dve.scalar_tensor_tensor(XC[:, ct, k:S], TR[b][:, c * S:(c + 1) * S - k], CWs[:, 3 - k, ct:ct + 1],
                                                         XC[:, ct, k:S], ALU.mult, ALU.add)
                        x = dve.drain()
                x.then_inc(s_trd, 1)

            def conv_out(m, o):
                dve.wait_ge(s_ct, m + 1)
                dve.scalar_tensor_tensor(o, TH[:, :, :], 1.0, XC[:, :, :], ALU.add, ALU.mult).then_inc(s_xs, 1)

            def gate(C, par, G, c0, n):
                take(C, par, G[:, 1, ds(c0, NC)], C + 1)
                dve.wait_ge(s_gt, n + 1)
                dve.tensor_scalar(G[:, :, ds(c0, NC)], G[:, :, ds(c0, NC)], 0.5, 0.5, ALU.mult, ALU.add)

            dve.drain().then_inc(s_xs, 1)
            dve.drain().then_inc(s_e3d, 1)
            with dve.Fori(0, NG) as i:
                C, e = C_AT + 4 * i, E_AT + PER_AT * i
                hk = {7: [lambda: take_rope(C, C_AT % 2, C + 1)],
                      SL_Q: [lambda: copy_t(e + EQ, QT(2, 4).rearrange("p (a s) -> p a s", a=2))],
                      15: [lambda: take(C + 1, (C_AT + 1) % 2, XR[:, 1, :], C + 2)],
                      SL_BC + 1: [lambda: conv(e + EBC)],
                      SL_BC + 2: [lambda: conv_out(i, BCT[:, ds(4 * i, 4), :])],
                      23: [lambda: gate(C + 2, C_AT % 2, GA, NC * i, 2 * i)],
                      31: [lambda: gate(C + 3, (C_AT + 1) % 2, GB, NC * i, 2 * i + 1)]}
                for r in range(4):
                    hk.setdefault(SL_PV[r], []).append(lambda r=r: head_out(4 * i + r, e + EPV[r]))
                for r in range(4):
                    hk.setdefault(SL_PT[r], []).append(lambda r=r: copy_probs(e + EPT[r]))
                for r in range(4):
                    hk.setdefault(SL_S[r], []).append(lambda r=r: maxima(4 * i + r))
                    hk.setdefault(SL_S[r] + 1, []).append(lambda r=r: scale_probs(4 * i + r))
                slots(dve, split_lo, C, 32, hk)

            def mult_gate(C, par, cols):
                dve.wait_ge(s_mm, 8 * C + 8)
                for t in range(2):
                    x = dve.tensor_tensor(GA[:, t, cols], acc[par][t][:, :], GA[:, t, cols], ALU.mult)
                x.then_inc(s_acc, 1)

            with dve.Fori(0, 2) as i:
                C = C_PA + 2 * i
                slots(dve, split_lo, C, 16, {7: [lambda: mult_gate(C, C_PA % 2, ds(2 * NC * i, NC))],
                                             15: [lambda: mult_gate(C + 1, (C_PA + 1) % 2, ds(2 * NC * i + NC, NC))]})

            def scan_sub(g, b):
                c, hb = b // 2, b % 2
                dve.wait_ge(s_dk, 4 * g + b + 1)
                dve.tensor_tensor(heads4(W[:, b, :]), heads4(X6[:, :]),
                                  ACS[:, c, ds(8 * g + 4 * hb, 4)].unsqueeze(2).broadcast_to([P, 4, P]), ALU.subtract).then_inc(s_sub, 1)

            def scan_w(g, b):
                dve.wait_ge(s_dx, 4 * g + b + 1)
                dve.tensor_tensor(heads4(W[:, b, :]), heads4(W[:, b, :]),
                                  CBB[:, b // 2, :].unsqueeze(1).broadcast_to([P, 4, P]), ALU.mult).then_inc(s_w, 1)

            def scan_first(g):
                dve.wait_ge(s_cb, g + 1)
                dve.tensor_copy(CBB[:, :, :].rearrange("p a l -> p (a l)"), X7[:, 0:3 * P]).then_inc(s_cbc, 1)
                scan_sub(g, 0)
                dve.wait_ge(s_zt, g + 1)
                dve.scalar_tensor_tensor(ZT[:, :, :], ZT[:, :, :], 1.0, ZR[:, :, :], ALU.add, ALU.mult)

            def scan_y0(g):
                dve.wait_ge(s_y0, g + 1)
                dve.wait_ge(s_xdd, 2 * g + 2)
                dve.tensor_tensor(Y[:, 0, :], X7[:, :], XD[:, 0, :], ALU.add).then_inc(s_y0d, 1)

            def scan_y1(g):
                dve.wait_ge(s_ey, g + 1)
                dve.tensor_tensor(heads8(XDS[:, :]), heads8(X6[:, :]),
                                  EA1[:, ds(8 * g, 8)].unsqueeze(2).broadcast_to([P, 8, SH]), ALU.mult)
                dve.tensor_tensor(Y[:, 1, :], X7[:, :], XD[:, 1, :], ALU.add)
                dve.drain()
                dve.tensor_tensor(Y[:, 1, :], Y[:, 1, :], XDS[:, :], ALU.add)
                dve.drain()
                dve.scalar_tensor_tensor(Y[:, :, :], Y[:, :, :], 0.5, ZT[:, :, :], ALU.mult, ALU.mult).then_inc(s_yg, 1)

            def scan_var(g):
                dve.wait_ge(s_ss, 2 * g + 4)
                dve.tensor_scalar(VV[:, 0:2], SS[:, 0:2], 1.0 / NC, EPS, ALU.mult, ALU.add).then_inc(s_v, 1)

            def scan_norm(g):
                dve.wait_ge(s_pow, g + 2)
                for t in range(2):
                    dve.tensor_scalar(Y[:, t, :], Y[:, t, :], RS[:, t:t + 1], None, ALU.mult)
                dve.drain().then_inc(s_yn, 1)

            def scan_hooks(g, k0):
                return {0: [lambda: scan_first(g)], 1: [lambda: scan_w(g, 0)], 2: [lambda: scan_sub(g, 1)],
                        3: [lambda: scan_w(g, 1)], 4: [lambda: scan_sub(g, 2)], 5: [lambda: scan_w(g, 2), lambda: scan_y0(g)],
                        6: [lambda: scan_sub(g, 3)], 7: [lambda: scan_w(g, 3)], 8: [lambda: scan_y1(g)],
                        10: [lambda: scan_var(g)], 11: [lambda: scan_norm(g)],
                        13: [lambda: dve_split_t(dve, g, LBh, LBl, k0, NWs, banks=(X6, X7), sa=s_e3a, done=s_e3d)]}

            def scan_inputs(t, e):
                dve.wait_ge(s_tra, 2 * e + 2)
                for c in range(2):
                    x = dve.tensor_tensor(heads8(XDT[:, c, :]), heads8(XTOK[:, c, :]),
                                          DT[:, c, ds(8 * t, 8)].unsqueeze(2).broadcast_to([P, 8, SH]), ALU.mult)
                x.then_inc(s_trd, 1)
                dve.drain()
                dve.tensor_tensor(heads8(XDS[:, :]), heads8(XDT[:, 0, :]),
                                  DST[:, ds(8 * t, 8)].unsqueeze(2).broadcast_to([P, 8, SH]), ALU.mult).then_inc(s_xd, 1)

            def scan_iteration(C, par, e, m, xa, t, g=None, k0=None):
                hk = scan_hooks(g, k0) if g is not None else {}
                hk[7] = hk.get(7, []) + [lambda: take(C, par, XR[:, 1, :], xa + 1)]
                hk[10] = hk.get(10, []) + [lambda: conv(e)]
                hk[12] = [lambda: conv_out(m, XC[:, :, :])]
                hk[13] = [lambda: scan_inputs(t, e + 1)] + hk.get(13, [])
                hk[15] = [lambda: take(C + 1, (par + 1) % 2, ZR[:, 1, :], xa + 2)]
                slots(dve, split_lo, C, 16, hk)

            def add_gated(C, par, cols, o):
                dve.wait_ge(s_mm, 8 * C + 8)
                for t in range(2):
                    x = dve.tensor_tensor(Y[:, t, :], acc[par][t][:, :], GB[:, t, cols], ALU.mult)
                x.then_inc(s_acc, 1)
                dve.drain()
                return dve.tensor_tensor(GA[:, :, cols] if o is None else o, GA[:, :, cols], Y[:, :, :], ALU.add)

            scan_iteration(C_X0, C_X0 % 2, E_X0, 4, XA_X0, 0)
            with dve.Fori(0, 4) as i:
                scan_iteration(C_L1 + 2 * i, C_L1 % 2, E_L1 + 2 * i, 5 + i, XA_X0 + 2 + 2 * i, i + 1, i, 4 * i)
            with dve.Fori(0, 2) as i:
                C = C_PB1 + 2 * i
                slots(dve, split_lo, C, 16, {7: [lambda: add_gated(C, C_PB1 % 2, ds(2 * NC * i, NC), None)],
                                             15: [lambda: add_gated(C + 1, (C_PB1 + 1) % 2, ds(2 * NC * i + NC, NC), None)]})
            with dve.Fori(0, 3) as i:
                scan_iteration(C_L2 + 2 * i, C_L2 % 2, E_L2 + 2 * i, 9 + i, XA_X0 + 10 + 2 * i, i + 5, i + 4, 4 * i)
            for s, v in scan_hooks(7, 12).items():
                for h in v:
                    h()
            for n in range(4):
                hk = {2: [lambda: dve_split_t(dve, E_PB2 + n - 1, LAh, LAl, 4 * n - 4)]} if n else {}
                hk[7] = [lambda: add_gated(C_PB2 + n, (C_PB2 + n) % 2, slice(NC * n, NC * n + NC), Y[:, :, :]).then_inc(s_mg, 1)]
                slots(dve, split_lo, C_PB2 + n, 8, hk)

            def add_residual(C, par, n):
                dve.wait_ge(s_mm, 8 * C + 8)
                for t in range(2):
                    x = dve.tensor_tensor(H[:, t, NC * n:NC * (n + 1)], acc[par][t][:, :], H[:, t, NC * n:NC * (n + 1)], ALU.add)
                x.then_inc(s_acc, 1)

            dve.wait_ge(s_hr, 32)
            for n in range(4):
                w = COLS[:, CN2 + 4 * n - 4:CN2 + 4 * n]
                slots(dve, split_lo, C_WO + n, 8,
                      {2: [lambda: dve_split_t(dve, E_WO + n - 1, LBh, LBl, 4 * n - 4, w) if n else
                           dve_split_t(dve, E_PB2 + 3, LAh, LAl, 12)],
                       7: [lambda: add_residual(C_WO + n, (C_WO + n) % 2, n)]})
            dve_split_t(dve, E_WO + 3, LBh, LBl, 12, COLS[:, CN2 + 12:CN2 + 16])
            dve.wait_ge(s_ss, SS_WO)
            dve.tensor_reduce(SS[:, 0:2], SS2[:, :, :], AX.X, ALU.add)
            dve.drain()
            dve.tensor_scalar(VV[:, 0:2], SS[:, 0:2], 1.0 / D, EPS, ALU.mult, ALU.add).then_inc(s_v, 1)
            dve.wait_ge(s_pow, 10)

            def mlp_rows(C, par, xa):
                dve.wait_ge(s_xa, xa)
                dve.tensor_scalar(XR[:, 1, :], acc[par][1][:, :], RS[:, 3:4], 0.0, ALU.mult, ALU.max).then_inc(s_acc, 1)
                dve.drain()
                dve.tensor_tensor(Y[:, :, :], XR[:, :, :], XR[:, :, :], ALU.mult).then_inc(s_ff, 1)

            def mlp(i, last=False):
                C, e = C_MLP + 8 * i, E_MLP + 4 * i
                hk = {}
                for k in range(4):
                    hk[8 * k + 7] = [lambda k=k: mlp_rows(C + k, (C_MLP + k) % 2, XA_UP + 4 * i + k + 1)]
                    hk[8 * k + 10] = [lambda k=k: dve_split_t(dve, e + k, LAh, LAl, 4 * k)]
                    hk[8 * k + 39] = [lambda k=k: add_residual(C + 4 + k, (C_MLP + k) % 2, k)]
                slots(dve, split_lo, C, 64, hk, last)

            with dve.Fori(0, 3) as i:
                mlp(i)
            mlp(3, last=True)
            dve.wait_ge(s_ss, SS_WO + 2)
            dve.tensor_scalar(VV[:, 0:2], SS[:, 0:2], 1.0 / D, EPS, ALU.mult, ALU.add).then_inc(s_v, 1)
            dve.wait_ge(s_pow, 11)
            dve.wait_ge(s_wf, 16)
            for t in range(2):
                dve.scalar_tensor_tensor(GB[:, t, :], H[:, t, :], RS[:, t:t + 1], GA[:, 0, :], ALU.mult, ALU.mult).then_inc(s_fin, 1)


_INS = ["x", "positions", "norm_mix_w", "w_in", "cmp_pos_k", "cmp_pos_v", "cmp_k_w1", "cmp_k_w2", "cmp_v_w1",
        "cmp_v_w2", "conv_w", "conv_b", "dt_bias", "a_log", "ssm_d", "ssm_norm_w", "w_proj_nsa", "w_proj_ssm",
        "w_out", "norm_mlp_w", "w_up", "w_down", "norm_final_w"]
_WHOLE = ("x", "positions", "norm_final_w")


def kernel(**inputs):
    import concourse.bacc as bacc
    from concourse.bass_utils import run_bass_kernel_spmd

    nc = bacc.Bacc("TRN2", target_bir_lowering=False, num_devices=1)
    arrays, args = {}, {}
    for name in _INS:
        v = np.ascontiguousarray(inputs[name])
        if name not in _WHOLE:
            v = v[0]
        arrays[name] = v
        args[name] = nc.dram_tensor(name, v.shape, mybir.dt.from_np(v.dtype), kind="ExternalInput").ap()
    inv = (np.float32(10000.0) ** (-np.arange(0, HD, 2, dtype=np.float32) / np.float32(HD))).astype(np.float32)
    arrays["inv_freq"] = inv
    args["inv_freq"] = nc.dram_tensor("inv_freq", inv.shape, F32, kind="ExternalInput").ap()
    out = nc.dram_tensor("out", (1, S, D), F32, kind="ExternalOutput").ap()
    build(nc, args, out)
    r = run_bass_kernel_spmd(nc, [arrays], core_ids=[0])
    return r.results[0]["out"]
```

```python
from contextlib import ExitStack

import numpy as np

import concourse.bass as bass
from concourse import mybir

F32 = mybir.dt.float32
F32R = mybir.dt.float32r
BF16 = mybir.dt.bfloat16
I32 = mybir.dt.int32
ALU = mybir.AluOpType
ACT = mybir.ActivationFunctionType
AX = mybir.AxisListType
ds = bass.ds

P = 128
S = 256
D = 2048
HD = 128
NH = 16
NG = 4
CMP, STR = 32, 16
NCMP = (S - CMP) // STR + 1
SCALE = float(HD) ** -0.5
NEG = -1e30
TINY = 1e-30
EPS = 1e-6
SG = 8
SH = 64
DI = 4096
XBCW = DI + 2 * SG * P
NC = 512
KT = 16
RING = 4
LEAD = 3
KC0, VC0, KS0, VS0, KW0, VW0 = (D + NC * i for i in range(6))
NG0 = D + 6 * NC
Z0 = NG0 + 3 * NH
XBC0 = Z0 + DI
DT0 = XBC0 + XBCW
GATE0 = DT0 + SH
SMALL = 3 * NH + SH
CN1, CSN, CN2, CCB, CCW, CPK, CPV = 0, 16, 48, 64, 112, 304, 336
C_SMALL, C_KC, C_VC, C_KS, C_VS, C_KW, C_VW, C_AT = 0, 1, 2, 3, 4, 5, 6, 7
C_PA = C_AT + 16
C_X0 = C_PA + 4
C_L1 = C_X0 + 2
C_PB1 = C_L1 + 8
C_L2 = C_PB1 + 4
C_PB2 = C_L2 + 6
C_WO = C_PB2 + 4
C_MLP = C_WO + 4
C_END = C_MLP + 32
E_U, E_KC, E_VC, E_KS, E_KW, E_AT = 0, 4, 5, 6, 7, 8
PER_AT = 10
EQ, EBC = 0, 3
EPT = (1, 4, 6, 8)
EPV = (2, 5, 7, 9)
E_X0 = E_AT + 4 * PER_AT
E_L1 = E_X0 + 2
E_L2 = E_L1 + 8
E_PB2 = E_L2 + 6
E_WO = E_PB2 + 4
E_MLP = E_WO + 4
SL_S, SL_PT, SL_PV = (12, 16, 20, 25), (16, 20, 25, 29), (17, 22, 27, 31)
SL_Q, SL_BC = 10, 18

N_SMALL = 16
XA_X0 = C_PA
XA_UP = XA_X0 + 16
SS_WO = 2 + 2 * SG + 8


def build(nc, a, out):
    ctx = ExitStack()
    with ctx:
        def sb(name, shape, dt=F32, c=ctx):
            return c.enter_context(nc.sbuf_tensor(name, shape, dt))

        def sem(name):
            return ctx.enter_context(nc.semaphore(name))

        acc = [[ctx.enter_context(nc.psum_tensor(f"acc{i}{t}", [P, NC], F32)) for t in range(2)] for i in range(2)]
        TR = [ctx.enter_context(nc.psum_tensor(f"tr{b}", [P, NC], F32)) for b in range(2)]
        X6 = ctx.enter_context(nc.psum_tensor("x6", [P, NC], F32))
        X7 = ctx.enter_context(nc.psum_tensor("x7", [P, NC], F32))

        raw = sb("raw", [P, RING, 2, NC])
        hi = sb("hi", [P, RING, 2, NC], F32R)
        lo = sb("lo", [P, RING, 2, NC], F32R)
        LAh = sb("LAh", [P, KT, S], F32R)
        LAl = sb("LAl", [P, KT, S], F32R)
        LBh = sb("LBh", [P, KT, S], F32R)
        LBl = sb("LBl", [P, KT, S], F32R)
        GA = sb("GA", [P, 2, D])
        GB = sb("GB", [P, 2, D])
        BCT = sb("BCT", [P, KT, S])
        H = BCT[:, :, :].rearrange("p a b -> p (a b)").rearrange("p (t n) -> p t n", t=2)
        XR = sb("XR", [P, 2, NC])
        Y = sb("Y", [P, 2, NC])
        COLS = sb("COLS", [P, 368])
        identf = sb("identf", [P, P])
        tri = sb("tri", [P, P])
        DAh = sb("DAh", [P, 2, SH], F32R)
        DT = sb("DT", [P, 2, SH])
        DA = sb("DA", [P, 2, SH])
        ACS = sb("ACS", [P, 2, SH])
        DST = sb("DST", [P, SH])
        EA1 = sb("EA1", [P, SH])
        DBC = sb("DBC", [P, SH])
        CWs = sb("CWs", [P, 5, 4])
        SS = sb("SS", [P, 16])
        SS2 = sb("SS2", [P, 2, 4])
        VV = sb("VV", [P, 4])
        RSX = sb("RSX", [P, 4])
        RS = sb("RS", [P, 4])
        mhalf = sb("mhalf", [P, 4])
        inv = sb("inv", [P, 4])

        s_raw = [sem(f"raw{i}") for i in range(RING)]
        s_hi = sem("hi_done")
        s_lo = sem("lo_done")
        s_mm = sem("group_multiplied")
        s_acc = sem("chunk_evacuated")
        s_xa = sem("act_half_evacuated")
        s_tr = sem("bank_transposed")
        s_tra = sem("event_read_by_act")
        s_trd = sem("event_read_by_dve")
        s_x = [sem(f"x_landed{n}") for n in range(4)]
        s_nw = sem("norm_weights_landed")
        s_small = sem("small_landed")
        s_const = sem("constants_made")
        s_w1 = [sem(f"compression_weights{n}_landed") for n in range(2)]
        s_w2 = sem("compression_second_weights_landed")
        s_smt = sem("gates_copied")
        s_colp = sem("cols_transposed")
        s_colc = sem("cols_copied")
        s_ss = sem("squares_summed")
        s_v = sem("variance_ready")
        s_pow = sem("rsqrt_ready")
        s_rx = sem("norm_factor_of_x_ready")
        s_cva = sem("conv_tiles_copied")
        s_cvp = sem("conv_taps_added")
        s_ang = sem("angles_ready")
        s_sin = sem("sines_ready")
        s_dts = sem("dt_steps_dve")
        s_dta = sem("dt_steps_act")
        s_acs = sem("cumulative_sums")
        s_rope = sem("rotated")
        s_xp = sem("compression_blocks_ready")
        s_hid = sem("compression_products")
        s_hta = sem("compression_tanh")
        s_hs = sem("compression_hidden_ready")
        s_kcr = sem("compressed_key_rotated")
        s_vcd = sem("compressed_values_copied")
        s_stage = sem("attention_operands_staged")
        s_sc = sem("scores_ready")
        s_nm = sem("maxima_ready")
        s_ex = sem("exponentials_ready")
        s_p = sem("probabilities_scaled")
        s_gt = sem("gate_tanh_ready")
        s_cw = sem("conv_weights_staged")
        s_ct = sem("conv_tanh_done")
        s_xs = sem("conv_output_ready")
        s_pg = sem("scan_operands_staged")
        s_xd = sem("scan_inputs_ready")
        s_xdd = sem("skip_term_ready")
        s_cb = sem("cb_products")
        s_cbc = sem("cb_copied")
        s_dk = sem("decay_sums")
        s_pl = sem("steps_spread")
        s_dx = sem("decay_ready")
        s_w = sem("scan_weights_ready")
        s_st = sem("state_product")
        s_stc = sem("state_copied")
        s_y0 = sem("first_chunk_product")
        s_y0d = sem("first_chunk_read")
        s_ey = sem("second_chunk_products")
        s_zt = sem("z_tanh_ready")
        s_yg = sem("gated_y_ready")
        s_yn = sem("normed_y_ready")
        s_e3 = sem("y_transposed")
        s_e3a = sem("y_read_by_act")
        s_e3d = sem("y_read_by_dve")
        s_mg = sem("merged_ready")
        s_hr = sem("residual_landed")
        s_ff = sem("mlp_rows_ready")
        s_hw = sem("residual_weighted")
        s_fin = [sem(f"output_ready{t}") for t in range(2)]
        s_wf = sem("final_weights_landed")
        s_out = sem("output_stored")

        w_in = a["w_in"].rearrange("(k p) c -> p k c", p=P)

        def load_chunk(sp, C, w, k0, c0, n=NC, extra=None):
            for j in range(8):
                sl = j % RING
                if not (isinstance(C, int) and 8 * C + j < RING):
                    sp.wait_ge(s_lo, 8 * C + j - RING + 1)
                for (src, cc, dst, m) in extra or [(w, c0, 0, n)]:
                    x = sp.dma_start(raw[:, sl, :, dst:dst + m], src[:, ds(k0 + 2 * j, 2), ds(cc, m)])
                    x.then_inc(s_raw[sl], 16)

        def split_hi(act, C, j):
            n = SMALL if isinstance(C, int) and C == 0 else NC
            sl = j % RING
            if isinstance(C, int) and C == 0:
                act.wait_ge(s_raw[sl], 32 * (j // RING + 1))
            else:
                act.wait_ge(s_raw[sl], 16 * (2 * C + j // RING + 1) + 32)
            if not (isinstance(C, int) and 8 * C + j < RING):
                act.wait_ge(s_mm, 8 * C + j - RING + 1)
            act.activation(hi[:, sl, :, 0:n], raw[:, sl, :, 0:n], ACT.Copy).then_inc(s_hi, 1)

        def split_lo(dve, C, j):
            n = SMALL if isinstance(C, int) and C == 0 else NC
            sl = j % RING
            dve.wait_ge(s_hi, 8 * C + j + 1)
            dve.tensor_tensor(lo[:, sl, :, 0:n], raw[:, sl, :, 0:n], hi[:, sl, :, 0:n].bitcast(F32),
                              ALU.subtract).then_inc(s_lo, 1)

        def slots(eng, split, C, n, hooks, last=False):
            for s in range(n):
                g = s + LEAD
                if not (last and g >= n):
                    split(eng, C + g // 8, g % 8)
                for h in hooks.get(s, ()):
                    h()

        def mm_chunk(pe, C, par, Lh, Ll, hooks, s0=0, need=None, n=NC):
            if not (isinstance(C, int) and C < 2):
                pe.wait_ge(s_acc, C - 1)
            for j in range(8):
                for (se, v) in (need or {}).get(j, ()):
                    pe.wait_ge(se, v)
                mm_group(pe, 8 * C + j, par, j, Lh, Ll, n)
                for h in hooks.get(s0 + j, ()):
                    h()

        def mm_group(pe, g, par, j, Lh, Ll, n=NC):
            sl = g % RING if isinstance(g, int) else j % RING
            pe.wait_ge(s_lo, g + 1)
            for kk in range(2):
                k = 2 * j + kk
                for t in range(2):
                    o = acc[par][t][:, 0:n]
                    xh, xl = Lh[:, k, t * P:(t + 1) * P], Ll[:, k, t * P:(t + 1) * P]
                    wh, wl = hi[:, sl, kk, 0:n], lo[:, sl, kk, 0:n]
                    pe.matmul(o, xh, wh, start=(k == 0), stop=False)
                    pe.matmul(o, xh, wl, start=False, stop=False)
                    x = pe.matmul(o, xl, wh, start=False, stop=(k == KT - 1))
            x.then_inc(s_mm, 1)

        def pe_event(pe, e, ready=()):
            if not (isinstance(e, int) and e == 0):
                pe.wait_ge(s_tra, 2 * e)
                pe.wait_ge(s_trd, e)
            for (se, v) in ready:
                pe.wait_ge(se, v)

        def pe_turn(pe, e, src, ready=(), banks=None, sm=None):
            if banks is None:
                pe_event(pe, e, ready)
            else:
                for (se, v) in ready:
                    pe.wait_ge(se, v)
            for b in range(2):
                for ct in (2 * b, 2 * b + 1):
                    for t in range(2):
                        x = pe.transpose((banks or TR)[b][:, (ct % 2) * S + t * P:(ct % 2) * S + (t + 1) * P],
                                         src[:, t, ct * P:(ct + 1) * P], identf[:, :])
                x.then_inc(sm or s_tr, 1)

        def act_split_t(act, e, Lh, k0, wc=None, banks=None, sm=None, done=None):
            for b in range(2):
                act.wait_ge(sm or s_tr, 2 * e + b + 1)
                for c in range(2):
                    ct = 2 * b + c
                    o = Lh[:, k0 + ct, :] if isinstance(k0, int) else Lh[:, ds(k0 + ct, 1), :]
                    src = (banks or TR)[b][:, c * S:(c + 1) * S]
                    if not isinstance(k0, int):
                        src = src.unsqueeze(1)
                    x = act.activation(o, src, ACT.Copy, scale=wc[:, ct:ct + 1] if wc is not None else 1.0)
                x.then_inc(done or s_tra, 1)

        def dve_split_t(dve, e, Lh, Ll, k0, wc=None, banks=None, sa=None, done=None):
            for b in range(2):
                dve.wait_ge(sa or s_tra, 2 * e + b + 1)
                for c in range(2):
                    ct = 2 * b + c
                    dyn = not isinstance(k0, int)
                    o = Ll[:, ds(k0 + ct, 1), :] if dyn else Ll[:, k0 + ct, :]
                    h = Lh[:, ds(k0 + ct, 1), :] if dyn else Lh[:, k0 + ct, :]
                    src = (banks or TR)[b][:, c * S:(c + 1) * S]
                    if dyn:
                        src = src.unsqueeze(1)
                    if wc is None:
                        x = dve.tensor_tensor(o, src, h.bitcast(F32), ALU.subtract)
                    else:
                        x = dve.scalar_tensor_tensor(o, src, wc[:, ct:ct + 1], h.bitcast(F32), ALU.mult, ALU.subtract)
            x.then_inc(done or s_trd, 1)


        XCT = sb("XCT", [P, 8, S])
        XC = XCT[:, 0:4, :]
        TH = XCT[:, 4:8, :]
        XP = XCT[:, :, :].rearrange("p a s -> p (a s)")[:, 0:CMP * NG * NCMP].rearrange(
            "p (i g j) -> p i g j", i=CMP, g=NG)
        early = BCT[:, :, :].rearrange("p a s -> p (a s)")
        used = [0]

        def view(size, pattern=None, **kw):
            v = early[:, used[0]:used[0] + size]
            used[0] += size
            assert used[0] <= KT * S
            return v.rearrange(pattern, **kw) if pattern else v

        NAT = view(5 * P, "p (n c) -> p n c", n=5)
        zz = view(P)
        ones = view(P)
        KV = view(NG * S, "p (g s) -> p g s", g=NG)
        HT = view(NG * NCMP)
        HS = view(NG * NCMP)
        KCN = view(2 * HD, "p (n d) -> p n d", n=2)[0:NG * NCMP, :, :]
        W2 = view(2 * HD, "p (n d) -> p n d", n=2)
        ROWS = view(3 * SH, "p (n h) -> p n h", n=3)
        SM = view(2 * SMALL, "p (t n) -> p t n", t=2)
        TM = view(10 * SH, "p (n t h) -> p n t h", n=5, t=2)
        ANG = view(3 * SH, "p (n h) -> p n h", n=3)
        KK = view(3 * SH, "p (n h) -> p n h", n=3)
        RR = Y[:, 0, 0:6 * SH].rearrange("p (f n h) -> p f n h", f=2, n=3)

        def QT(r0, r1):
            t, b = r0 // 2, r0 % 2
            return GB[:, t, D - NC + b * S:D - NC + (b + r1 - r0) * S]

        def V_(t, b):
            return V3[:, 2 * t + b, :] if t + b < 2 else GA[:, 1, D - NC:D]

        VCB = GA[0:NCMP, 0, D - NC:D].rearrange("p (g d) -> p g d", g=NG)
        flat_y = Y[:, :, :].rearrange("p t n -> p (t n)")
        PTS = flat_y[:, 0:768].rearrange("p (n q) -> p n q", n=2)
        PTC = flat_y[0:NCMP, 768:1024].rearrange("p (n q) -> p n q", n=2)

        pre = ExitStack()
        TAB = sb("TAB", [P, 2, 3, P], c=pre)
        KT_ = sb("KT", [P, 2, NG, S], c=pre)
        V3 = sb("V", [P, 3, NC], c=pre)
        PB = sb("PB", [P, 768], c=pre)
        VSs = sb("VSs", [P, 2, 2, HD], c=pre)
        KCT = sb("KCT", [P, NG, NCMP], c=pre)
        VCs = sb("VCs", [NCMP, HD], c=pre)
        identb = sb("identb", [P, P], BF16, c=pre)
        maskq = sb("maskq", [P, P], BF16, c=pre)
        GR = sb("GR", [P, NH, 6], c=pre)
        MX = sb("MX", [P, 6], c=pre)
        NM = sb("NM", [P, 6], c=pre)
        SUM = sb("SUM", [P, 6], c=pre)
        SCB = sb("SCB", [P, 2, NCMP], c=pre)
        EC = sb("EC", [P, 2, NCMP], c=pre)
        PC = sb("PC", [P, 2, NCMP], c=pre)
        CM1 = sb("CM1", [P, 2, NCMP], c=pre)
        CNEG = sb("CNEG", [P, 2, NCMP], c=pre)
        POSI = sb("POSI", [P, 3], I32, c=pre)
        POS = sb("POS", [P, 3], c=pre)
        pre.close()
        post = ExitStack()
        XTOK = sb("XTOK", [P, 2, NC], c=post)
        XDT = sb("XDT", [P, 2, NC], c=post)
        XDS = Y[:, 1, :]
        BTg = Y[:, 0, 0:S]
        CTg = sb("CTg", [P, S], c=post)
        SU = sb("SU", [P, P], F32R, c=post)
        MH = sb("MH", [P, NC], F32R, c=post)
        ML = sb("ML", [P, NC], F32R, c=post)
        NWs = sb("NWs", [P, 4], c=post)
        W = sb("W", [P, 4, NC], c=post)
        ZT = sb("ZT", [P, 2, NC], c=post)
        post.close()
        flat_th = TH.rearrange("p a s -> p (a s)")
        CBB = flat_th[:, 0:3 * P].rearrange("p (n l) -> p n l", n=3)
        ST = flat_th[:, NC:2 * NC]
        XD = XTOK
        MG = (Y, XR)
        ZR = XR
        block = ctx.enter_context(nc.Block())

        def last_hooks(hooks):
            last = {12: 11, 13: 11}
            return {last.get(s, s): h for s, h in hooks.items()}

        def heads4(x):
            return x.rearrange("p (h d) -> p h d", h=4)

        def heads8(x):
            return x.rearrange("p (h d) -> p h d", h=8)

        w1v = (GA, GB)
        UB = (TR, acc[1])
        SMT = Y[0:SMALL, 1, 0:S]
        x_rows = a["x"][0].rearrange("(t p) d -> p t d", p=P)
        out_rows = out[0].rearrange("(t p) d -> p t d", p=P)

        PAIR = [(c, j) for c in range(2) for j in range(6)] + [(c, j) for c in range(2) for j in (6, 7)]

        @block.sync
        def _(sp):
            for n in range(4):
                sp.dma_start(GA[:, :, NC * n:NC * (n + 1)], x_rows[:, :, NC * n:NC * (n + 1)]).then_inc(s_x[n], 16)
            w_na = a["w_proj_nsa"].rearrange("(k p) c -> p k c", p=P)
            w_ss = a["w_proj_ssm"].rearrange("(k p) c -> p k c", p=P)
            w_ou = a["w_out"].rearrange("(k p) c -> p k c", p=P)
            w_up = a["w_up"].rearrange("(k p) c -> p k c", p=P)
            w_dn = a["w_down"].rearrange("(k p) c -> p k c", p=P)
            load_chunk(sp, C_SMALL, w_in, 0, 0, extra=[(w_in, NG0, 0, 3 * NH), (w_in, DT0, 3 * NH, SH)])
            for C, c0 in ((C_KC, KC0), (C_VC, VC0), (C_KS, KS0), (C_VS, VS0), (C_KW, KW0), (C_VW, VW0)):
                load_chunk(sp, C, w_in, 0, c0)
            with sp.Fori(0, NG) as i:
                for k, c0 in enumerate((0, XBC0 + DI, GATE0, GATE0 + D)):
                    load_chunk(sp, C_AT + 4 * i + k, w_in, 0, c0 + NC * i)
            with sp.Fori(0, 2) as i:
                for k in range(2):
                    load_chunk(sp, C_PA + 2 * i + k, w_na, 0, 2 * NC * i + NC * k)
            load_chunk(sp, C_X0, w_in, 0, XBC0)
            load_chunk(sp, C_X0 + 1, w_in, 0, Z0)
            with sp.Fori(0, 4) as i:
                load_chunk(sp, C_L1 + 2 * i, w_in, 0, XBC0 + NC + NC * i)
                load_chunk(sp, C_L1 + 2 * i + 1, w_in, 0, Z0 + NC + NC * i)
            with sp.Fori(0, 2) as i:
                for k in range(2):
                    load_chunk(sp, C_PB1 + 2 * i + k, w_ss, 0, 2 * NC * i + NC * k)
            with sp.Fori(0, 3) as i:
                load_chunk(sp, C_L2 + 2 * i, w_in, 0, XBC0 + 5 * NC + NC * i)
                load_chunk(sp, C_L2 + 2 * i + 1, w_in, 0, Z0 + 5 * NC + NC * i)
            for s, (c, j) in enumerate(PAIR):
                sp.wait_ge(s_lo, 8 * C_PB2 + s - RING + 1)
                sp.dma_start(raw[:, s % RING, :, :],
                             w_ss[:, KT + 2 * j:KT + 2 * j + 2, NC * c:NC * (c + 1)]).then_inc(s_raw[s % RING], 16)
            for n in range(2, 4):
                load_chunk(sp, C_PB2 + n, w_ss, KT, NC * n)
            for n in range(4):
                load_chunk(sp, C_WO + n, w_ou, 0, NC * n)
            with sp.Fori(0, 4) as i:
                for k in range(4):
                    load_chunk(sp, C_MLP + 8 * i + k, w_up, 0, D * i + NC * k)
                for k in range(4):
                    load_chunk(sp, C_MLP + 8 * i + 4 + k, w_dn, KT * i, NC * k)
            for n in range(2):
                cols = slice(D // 2 * n, D // 2 * (n + 1))
                for t in (1, 0):
                    sp.wait_ge(s_fin[t], n + 1)
                    sp.dma_start(out_rows[:, t, cols], GB[:, t, cols]).then_inc(s_out, 16)
            sp.wait_ge(s_out, 64)

        @block.gpsimd
        def _(pool):
            def rms(n, width, o):
                pool.wait_ge(s_ss, n)
                pool.tensor_tensor(VV[:, 0:2], SS[:, 0:2], inv[:, 0:2] if width == D else inv[:, 2:4], ALU.mult)
                pool.drain()
                pool.tensor_scalar(VV[:, 0:2], VV[:, 0:2], EPS, None, ALU.add)
                pool.drain()
                pool.tensor_tensor(o, VV[:, 0:2], mhalf[:, 0:2], ALU.pow)
                pool.drain().then_inc(s_pow, 1)

            pool.memset(identf[:, :], 0.0)
            pool.memset(zz[:, :], 0.0)
            pool.memset(ones[:, :], 1.0)
            pool.memset(mhalf[:, :], -0.5)
            pool.memset(inv[:, 0:2], 1.0 / D)
            pool.memset(inv[:, 2:4], 1.0 / NC)
            pool.memset(POSI[:, :], 0)
            pool.drain()
            pool.affine_select(identf[:, :], identf[:, :], [[-1, P]], ALU.not_equal, 1.0, base=0, channel_multiplier=1)
            pool.affine_select(tri[:, :], ones[:, :], [[1, P]], ALU.is_ge, 0.0, base=0, channel_multiplier=-1)
            pool.affine_select(maskq[:, :], zz[:, :], [[-1, P]], ALU.is_ge, NEG, base=0, channel_multiplier=1)
            cm = [[P, 2], [-STR, NCMP]]
            one30 = ones[:, 0:2 * NCMP].rearrange("p (t j) -> p t j", t=2)
            zero30 = zz[:, 0:2 * NCMP].rearrange("p (t j) -> p t j", t=2)
            pool.affine_select(CM1[:, :, :], one30, cm, ALU.is_ge, 0.0, base=1 - CMP, channel_multiplier=1)
            pool.affine_select(CNEG[:, :, :], zero30, cm, ALU.is_ge, NEG, base=1 - CMP, channel_multiplier=1)
            pool.drain().then_inc(s_const, 1)
            small = [
                (NAT[0:32, 0, :], a["ssm_norm_w"].rearrange("(k p) -> k p", p=P)),
                (NAT[32:48, 0, :], a["norm_mlp_w"].rearrange("(k p) -> k p", p=P)),
                (NAT[48:96, 0, :], a["conv_b"].rearrange("(k p) -> k p", p=P)),
                (NAT[0:96, 1, :], a["conv_w"].rearrange("i (k p) -> (i k) p", p=P)[0:96, :]),
                (NAT[0:96, 2, :], a["conv_w"].rearrange("i (k p) -> (i k) p", p=P)[96:192, :]),
                (NAT[0:32, 3, :], a["cmp_pos_k"]),
                (NAT[32:64, 3, :], a["cmp_pos_v"]),
                (ROWS[:, 0, :], a["dt_bias"].partition_broadcast(P)),
                (ROWS[:, 1, :], a["a_log"].partition_broadcast(P)),
                (ROWS[:, 2, :], a["inv_freq"].partition_broadcast(P)),
                (DBC[:, :], a["ssm_d"].partition_broadcast(P)),
                (POSI[:, 0:2], a["positions"][0].rearrange("(t p) -> p t", p=P)),
            ] + [(POSI[NCMP * g:NCMP * (g + 1), 2:3],
                  a["positions"][0][STR:S].rearrange("(j i) -> j i", i=STR)[:, STR - 1:STR]) for g in range(NG)]
            for o, i_ in small:
                pool.dma_start(o, i_, allow_slow_non_contiguous=True).then_inc(s_small, 16)
            assert len(small) == N_SMALL
            rms(2, D, RSX[:, 0:2])
            pool.tensor_scalar(RSX[:, 2:4], RSX[:, 0:2], 0.5, None, ALU.mult).then_inc(s_rx, 1)
            pool.wait_ge(s_trd, 4)
            for n, w in enumerate(("cmp_k_w1", "cmp_v_w1")):
                for q in range(4):
                    pool.wait_ge(s_lo, 8 * n + 2 * q + 6)
                    i0, i1 = CMP // 4 * q, CMP // 4 * (q + 1)
                    pool.dma_start(w1v[n][:, :, :].rearrange("p t n -> p (t n)").rearrange("p (i h) -> p i h", i=CMP)[:, i0:i1, :],
                                   a[w].rearrange("(i d) h -> d i h", d=P)[:, i0:i1, :]).then_inc(s_w1[n], 16)
            for n, w in enumerate(("cmp_k_w2", "cmp_v_w2")):
                pool.dma_start(W2[:, n, :], a[w]).then_inc(s_w2, 16)

            def stage_conv(m, tile):
                pool.wait_ge(s_cvp, m + 1)
                taps = COLS[:, CCW:CCW + 192].rearrange("p (i t) -> p i t", i=4)
                pool.tensor_copy(CWs[:, 0:4, :], taps[:, :, ds(tile, 4)]).then_inc(s_cw, 1)
                pool.tensor_copy(CWs[:, 4, :], COLS[:, ds(tile + CCB, 4)]).then_inc(s_cw, 1)

            pool.wait_ge(s_kcr, 2)
            pool.wait_ge(s_vcd, 1)
            pool.wait_ge(s_acc, C_AT)
            with pool.Fori(0, NG) as i:
                e = E_AT + PER_AT * i
                pool.wait_ge(s_tr, 2 * e)
                pool.wait_ge(s_tra, 2 * e)
                pool.wait_ge(s_trd, e)
                for kt in range(2):
                    for b in range(2):
                        pool.tensor_copy(VSs[:, kt, b, :], V_(kt, b)[:, ds(HD * i, HD)]).then_inc(s_stage, 1)
                pool.tensor_copy(VCs[:, :].unsqueeze(1), VCB[:, ds(i, 1), :]).then_inc(s_stage, 1)
                stage_conv(i, 32 + 4 * i)

            def stage_scan(g):
                pool.wait_ge(s_e3d, g + 1)
                pool.tensor_copy(BTg[:, :].unsqueeze(1), BCT[:, ds(g, 1), :]).then_inc(s_pg, 1)
                pool.tensor_copy(CTg[:, :].unsqueeze(1), BCT[:, ds(g + 8, 1), :]).then_inc(s_pg, 1)
                pool.tensor_copy(NWs[:, :], COLS[:, ds(4 * g + CSN, 4)]).then_inc(s_pg, 1)

            def spread(g, b):
                c, hb = b // 2, b % 2
                if b:
                    pool.wait_ge(s_dk, 4 * g + b)
                for o, da in ((MH, DAh), (ML, DA)):
                    v = da[:, c, ds(8 * g + 4 * hb, 4)]
                    if da is DAh:
                        v = v.bitcast(F32)
                    pool.tensor_tensor(heads4(o[:, :]), tri[:, :].unsqueeze(1).broadcast_to([P, 4, P]),
                                       v.unsqueeze(2).broadcast_to([P, 4, P]), ALU.mult).then_inc(s_pl, 1)

            def skip_term(g, e):
                pool.wait_ge(s_trd, e + 1)
                for t in range(2):
                    pool.tensor_tensor(heads8(XD[:, t, :]), heads8(XTOK[:, t, :]),
                                       DBC[:, ds(8 * g, 8)].unsqueeze(2).broadcast_to([P, 8, SH]),
                                       ALU.mult).then_inc(s_xdd, 1)

            pool.wait_ge(s_trd, E_X0)
            pool.wait_ge(s_tra, 2 * E_X0)

            pool.tensor_scalar(SU[:, :], tri[:, :], -1.0, 1.0, ALU.mult, ALU.add)
            pool.drain()

            def scan_iteration(t, m, e):
                if not (isinstance(t, int) and t == 0):
                    for b in (1, 2, 3):
                        spread(t - 1, b)
                stage_conv(m, 4 * t)
                if not (isinstance(t, int) and t == 0):
                    rms(2 + 2 * t, NC, RS[:, 0:2])
                stage_scan(t)
                spread(t, 0)
                skip_term(t, e + 1)

            scan_iteration(0, 4, E_X0)
            with pool.Fori(0, 4) as i:
                scan_iteration(1 + i, 5 + i, E_L1 + 2 * i)
            with pool.Fori(0, 3) as i:
                scan_iteration(5 + i, 9 + i, E_L2 + 2 * i)
            for b in (1, 2, 3):
                spread(7, b)
            rms(18, NC, RS[:, 0:2])
            pool.wait_ge(s_pg, 24)
            for t in range(2):
                pool.dma_start(H[:, t, :], x_rows[:, t, :]).then_inc(s_hr, 16)
            pool.wait_ge(s_mg, 4)
            pool.dma_start(GA[:, 0, :], a["norm_final_w"].partition_broadcast(P)).then_inc(s_wf, 16)
            for n, o in ((1, RS[:, 2:4]), (2, RS[:, 0:2])):
                pool.wait_ge(s_v, n)
                pool.tensor_tensor(o, VV[:, 0:2], mhalf[:, 0:2], ALU.pow).then_inc(s_pow, 1)

        @block.tensor
        def _(pe):
            pe.wait_ge(s_const, 1)
            pe.wait_ge(s_nw, 16)
            pe.transpose(X6[:, 0:16], NAT[0:16, 4, :], identf[0:16, 0:16]).then_inc(s_colp, 1)
            for n in range(4):
                free = [(s_tra, 2 * n - 2), (s_trd, n - 1)] if n > 1 else []
                pe_turn(pe, E_U + n, GA[:, :, NC * n:NC * (n + 1)], [(s_x[n], 16)] + free, banks=UB[n % 2], sm=s_tr)
            for j in range(8):
                if j % 2 == 0:
                    pe.wait_ge(s_trd, j // 2 + 1)
                pe.wait_ge(s_lo, j + 1)
                for k in (2 * j, 2 * j + 1):
                    wh, wl = hi[:, j % RING, k % 2, 0:SMALL], lo[:, j % RING, k % 2, 0:SMALL]
                    o = acc[0][0][0:SMALL, 0:S]
                    pe.matmul(o, wh, LAh[:, k, :], start=(k == 0), stop=False)
                    pe.matmul(o, wh, LAl[:, k, :], start=False, stop=False)
                    x = pe.matmul(o, wl, LAh[:, k, :], start=False, stop=(k == KT - 1))
                x.then_inc(s_mm, 1)

            def turn_columns():
                pe.wait_ge(s_small, 16 * N_SMALL)
                pe.wait_ge(s_colc, 1)
                for n, (r, c) in enumerate(((96, 16), (96, 112), (96, 208), (64, 304))):
                    x = pe.transpose(X6[:, c:c + r], NAT[0:r, n, :], identf[0:r, 0:r])
                x.then_inc(s_colp, 1)

            def turn_small():
                pe.wait_ge(s_smt, 1)
                for t in range(2):
                    x = pe.transpose(acc[0][1][:, SMALL * t:SMALL * (t + 1)], SMT[:, t * P:(t + 1) * P],
                                     identf[0:SMALL, 0:SMALL])
                x.then_inc(s_smt, 1)


            def cumsum():
                pe.wait_ge(s_dts, 2)
                da = DA[:, :, :].rearrange("p t h -> p (t h)")
                pe.wait_ge(s_colc, 2)
                pe.matmul(X6[:, 0:P], tri[:, :], da, start=True, stop=True)
                pe.matmul(X6[:, P:2 * P], ones[:, :], da, start=True, stop=True).then_inc(s_acs, 1)

            def compress(n):
                pe.wait_ge(s_xp, n + 1)
                pe.wait_ge(s_w1[n], 64)
                w = w1v[n][:, :, :].rearrange("p t n -> p (t n)")
                for i in range(CMP):
                    x = pe.matmul(X7[:, 0:NG * NCMP], w[:, HD * i:HD * (i + 1)],
                                  XP[:, i, :, :].rearrange("p g j -> p (g j)"), start=(i == 0), stop=(i == CMP - 1))
                x.then_inc(s_hid, 1)

            def compress_k2():
                pe.wait_ge(s_hs, 1)
                pe.wait_ge(s_w2, 32)
                pe.wait_ge(s_dts, 3)
                pe.matmul(X6[0:NG * NCMP, 0:HD], HS[:, :], W2[:, 0, :], start=True, stop=True).then_inc(s_hid, 1)

            def compress_k3():
                pe.wait_ge(s_kcr, 1)
                n = NG * NCMP
                pe.transpose(X6[:, P:P + n], KCN[:, 0, :], identf[0:n, 0:n]).then_inc(s_hid, 1)

            def compress_v2():
                pe.wait_ge(s_hs, 2)
                pe.wait_ge(s_kcr, 2)
                for g in range(NG):
                    x = pe.matmul(X6[0:NCMP, HD * g:HD * (g + 1)], HS[:, NCMP * g:NCMP * (g + 1)], W2[:, 1, :],
                                  start=True, stop=True)
                x.then_inc(s_hid, 1)

            mm_chunk(pe, C_KC, 1, LAh, LAl, {0: [turn_small], 1: [turn_columns], 6: [cumsum]})
            mm_chunk(pe, C_VC, 0, LAh, LAl, {2: [lambda: pe_turn(pe, E_KC, XR, [(s_acc, C_KC + 1)])],
                                             6: [lambda: compress(0)]})
            mm_chunk(pe, C_KS, 1, LAh, LAl, {0: [compress_k2],
                                             2: [lambda: pe_turn(pe, E_VC, XR, [(s_acc, C_VC + 1)])],
                                             4: [compress_k3], 6: [lambda: compress(1)]})
            mm_chunk(pe, C_VS, 0, LAh, LAl, {0: [compress_v2],
                                             2: [lambda: pe_turn(pe, E_KS, Y, [(s_rope, 1)])]})
            mm_chunk(pe, C_KW, 1, LAh, LAl, {})
            mm_chunk(pe, C_VW, 0, LAh, LAl, {2: [lambda: pe_turn(pe, E_KW, Y, [(s_rope, 2)])]})

            def scores(i, r, e):
                n = 4 * i + r
                pe.wait_ge(s_tra, 2 * e + 2)
                pe.wait_ge(s_trd, e + 1)
                pe.wait_ge(s_stage, 5 * i + 5)
                pe.wait_ge(s_ex, n + 1)
                q0, q1 = QT(r, r + 1)[:, 0:P], QT(r, r + 1)[:, P:S]
                for b in range(2):
                    pe.matmul(X6[:, b * S + P:b * S + S], identb[:, :], maskq[:, :], start=(b == 0), stop=False,
                              skip_group_check=True)
                for b in range(2):
                    pe.matmul(X6[:, b * S:(b + 1) * S], q1, KT_[:, b, ds(i, 1), :].rearrange("p o s -> p (o s)"), start=False, stop=(b == 1),
                              skip_group_check=True)
                pe.matmul(X7[:, 0:S].rearrange("p (b k) -> p b k", b=2), identb[:, :],
                          maskq[:, :].unsqueeze(1).broadcast_to([P, 2, P]), start=True, stop=False, skip_group_check=True)
                for b in range(2):
                    pe.matmul(X7[:, b * P:(b + 1) * P], q0, KT_[:, b, ds(i, 1), 0:P].rearrange("p o s -> p (o s)"), start=False, stop=False, skip_group_check=True)
                for t, q in enumerate((q0, q1)):
                    x = pe.matmul(X7[:, S + NCMP * t:S + NCMP * (t + 1)], q, KCT[:, ds(i, 1), :].rearrange("p o s -> p (o s)"), start=False, stop=(t == 1),
                                  skip_group_check=True)
                x.then_inc(s_sc, 1)

            def turn_probs(i, r, e):
                pe_event(pe, e, [(s_p, 4 * i + r + 1)])
                for b in range(2):
                    pe.transpose(TR[b][:, 0:P], PB[:, 512 + P * b:512 + P * (b + 1)], identf[:, :])
                    for k in range(2):
                        pe.transpose(TR[b][:, P * (k + 1):P * (k + 2)], PB[:, S * b + P * k:S * b + P * (k + 1)], identf[:, :])
                    pe.transpose(TR[b][0:NCMP, 384:512], PC[:, b, :], identf[:, :]).then_inc(s_tr, 1)

            def values(i, r, e):
                pe_event(pe, e)
                for b in range(2):
                    pe.matmul(TR[0][:, 0:S], VSs[:, 0, b, :], PTS[:, b, 0:S], start=(b == 0), stop=False,
                              skip_group_check=True)
                    x = pe.matmul(TR[0][:, P:S], VSs[:, 1, b, :], PTS[:, b, S:384], start=False, stop=False,
                                  skip_group_check=True)
                x.then_inc(s_tr, 1)
                pe.matmul(TR[0][:, 0:S], VCs[:, :], PTC[:, :, :].rearrange("p t q -> p (t q)"), start=False, stop=True,
                          skip_group_check=True).then_inc(s_tr, 1)

            with pe.Fori(0, NG) as i:
                C, e = C_AT + 4 * i, E_AT + PER_AT * i
                hooks = {SL_Q: [lambda: pe_turn(pe, e + EQ, Y, [(s_rope, i + 3)])],
                         SL_BC: [lambda: pe_turn(pe, e + EBC, XR, [(s_acc, C + 2)])]}
                for r in range(4):
                    hooks.setdefault(SL_PV[r], []).append(lambda r=r: values(i, r, e + EPV[r]))
                for r in range(4):
                    hooks.setdefault(SL_PT[r], []).append(lambda r=r: turn_probs(i, r, e + EPT[r]))
                for r in range(4):
                    hooks.setdefault(SL_S[r], []).append(lambda r=r: scores(i, r, e))
                for k in range(4):
                    mm_chunk(pe, C + k, (C_AT + k) % 2, LAh, LAl,
                             {s - 8 * k: v for s, v in hooks.items() if s // 8 == k})
            with pe.Fori(0, 2) as i:
                for k in range(2):
                    mm_chunk(pe, C_PA + 2 * i + k, (C_PA + k) % 2, LBh, LBl, {}, need={7: [(s_trd, E_X0)]})

            def scan_cb(g):
                pe.wait_ge(s_pg, 3 * g + 3)
                pe.wait_ge(s_e3d, g + 1)
                pe.transpose(X7[:, 2 * P:3 * P], BTg[:, 0:P], identf[:, :])
                for c in range(2):
                    x = pe.matmul(X7[:, c * P:(c + 1) * P], BTg[:, c * P:(c + 1) * P], CTg[:, c * P:(c + 1) * P],
                                  start=True, stop=True)
                x.then_inc(s_cb, 1)

            def scan_decay(g, b):
                pe.wait_ge(s_pl, 8 * g + 2 * b + 2)
                if b:
                    pe.wait_ge(s_dx, 4 * g + b)
                pe.matmul(X6[:, :], SU[:, :], MH[:, :], start=True, stop=False)
                pe.matmul(X6[:, :], SU[:, :], ML[:, :], start=False, stop=True).then_inc(s_dk, 1)

            def scan_state(g):
                pe.wait_ge(s_cbc, g + 1)
                pe.wait_ge(s_xd, g + 1)
                pe.matmul(X7[:, :], CBB[:, 2, :], XDS[:, :], start=True, stop=True).then_inc(s_st, 1)

            def scan_y(c):
                for h in range(8):
                    x = pe.matmul(X7[:, h * SH:(h + 1) * SH], W[:, 2 * c + h // 4, (h % 4) * P:(h % 4 + 1) * P],
                                  XDT[:, c, h * SH:(h + 1) * SH], start=True, stop=True)
                return x

            def scan_y0(g):
                pe.wait_ge(s_stc, g + 1)
                pe.wait_ge(s_w, 4 * g + 2)
                scan_y(0).then_inc(s_y0, 1)

            def scan_y1(g):
                pe.wait_ge(s_y0d, g + 1)
                pe.wait_ge(s_w, 4 * g + 4)
                pe.matmul(X6[:, :], CTg[:, P:S], ST[:, :], start=True, stop=True)
                scan_y(1).then_inc(s_ey, 1)

            def scan_turn_y(g):
                pe_turn(pe, None, Y, [(s_yn, g + 1)], banks=(X6, X7), sm=s_e3)

            def scan_hooks(g):
                return {0: [lambda: scan_cb(g), lambda: scan_decay(g, 0)], 2: [lambda: scan_decay(g, 1)],
                        3: [lambda: scan_state(g)], 4: [lambda: scan_decay(g, 2)], 5: [lambda: scan_y0(g)],
                        6: [lambda: scan_decay(g, 3)], 8: [lambda: scan_y1(g)], 12: [lambda: scan_turn_y(g)]}

            def turn_back(e, m):
                pe_event(pe, e, [(s_xs, m + 2)])
                for t in range(2):
                    for ct in range(4):
                        x = pe.transpose(TR[t][:, ct * P:(ct + 1) * P], XC[:, ct, t * P:(t + 1) * P], identf[:, :])
                    x.then_inc(s_tr, 1)

            def scan_iteration(C, par, e, m, g=None):
                hooks = scan_hooks(g) if g is not None else {}
                hooks[8] = hooks.get(8, []) + [lambda: pe_turn(pe, e, XR, [(s_acc, C + 1)])]
                hooks[15] = [lambda: turn_back(e + 1, m)]
                for k in range(2):
                    mm_chunk(pe, C + k, (par + k) % 2, LAh, LAl, {s - 8 * k: v for s, v in hooks.items() if s // 8 == k})

            scan_iteration(C_X0, C_X0 % 2, E_X0, 4)
            with pe.Fori(0, 4) as i:
                scan_iteration(C_L1 + 2 * i, C_L1 % 2, E_L1 + 2 * i, 5 + i, i)
            with pe.Fori(0, 2) as i:
                for k in range(2):
                    mm_chunk(pe, C_PB1 + 2 * i + k, (C_PB1 + k) % 2, LBh, LBl, {}, need={0: [(s_e3d, 5)]})
            with pe.Fori(0, 3) as i:
                scan_iteration(C_L2 + 2 * i, C_L2 % 2, E_L2 + 2 * i, 9 + i, i + 4)
            hooks = last_hooks(scan_hooks(7))
            hooks[15] = [lambda: pe_turn(pe, E_PB2, MG[0], [(s_mg, 1)])]
            pe.wait_ge(s_acc, C_PB2 - 1)
            for s, (c, j) in enumerate(PAIR):
                if s == 6:
                    pe.wait_ge(s_acc, C_PB2)
                if s == 12:
                    pe.wait_ge(s_e3d, 9)
                mm_group(pe, 8 * C_PB2 + s, (C_PB2 + c) % 2, j, LBh, LBl)
                for h in hooks.get(s, ()):
                    h()
            for n in range(2, 4):
                hooks = {2: [lambda: pe_turn(pe, E_PB2 + n - 1, MG[(n - 1) % 2], [(s_mg, n)])]}
                mm_chunk(pe, C_PB2 + n, (C_PB2 + n) % 2, LBh, LBl, hooks)
            for n in range(4):
                hooks = ({2: [lambda: pe_turn(pe, E_WO + n - 1, H[:, :, NC * (n - 1):NC * n], [(s_acc, C_WO + n)])]} if n
                         else {2: [lambda: pe_turn(pe, E_PB2 + 3, MG[1], [(s_mg, 4)])]})
                mm_chunk(pe, C_WO + n, (C_WO + n) % 2, LAh, LAl, hooks, need={6: [(s_trd, E_PB2 + 4)]})
            pe_turn(pe, E_WO + 3, H[:, :, 3 * NC:4 * NC], [(s_acc, C_WO + 4)])
            with pe.Fori(0, 4) as i:
                C, e = C_MLP + 8 * i, E_MLP + 4 * i
                for k in range(4):
                    hooks = {2: [lambda: pe_turn(pe, e + k - 1, Y, [(s_ff, 4 * i + k)])]} if k else {}
                    mm_chunk(pe, C + k, (C_MLP + k) % 2, LBh, LBl, hooks, need={6: [(s_trd, E_MLP)]})
                for k in range(4):
                    hooks = {} if k else {2: [lambda: pe_turn(pe, e + 3, Y, [(s_ff, 4 * i + 4)])]}
                    mm_chunk(pe, C + 4 + k, (C_MLP + k) % 2, LAh, LAl, hooks, need={6: [(s_trd, e + 4)]})

        @block.scalar
        def _(act):
            def take(C, par, o, n=NC, func=ACT.Copy, scale=RSX[:, 0:1]):
                act.wait_ge(s_mm, 8 * C + 8)
                act.activation(o, acc[par][0][:, 0:n], func, scale=scale).then_inc(s_xa, 1)

            def copy_t(e, o):
                act.wait_ge(s_tr, 2 * e + 1)
                act.activation(o, TR[0][:, :].rearrange("p (a s) -> p a s", a=2), ACT.Copy).then_inc(s_tra, 2)

            act.dma_start(NAT[0:16, 4, :], a["norm_mix_w"].rearrange("(k p) -> k p", p=P)).then_inc(s_nw, 16)
            act.wait_ge(s_colc, 1)
            for n in range(4):
                act_split_t(act, E_U + n, LAh, 4 * n, COLS[:, CN1 + 4 * n:CN1 + 4 * n + 4], banks=UB[n % 2])
                if n == 1:
                    for j in range(LEAD):
                        split_hi(act, C_SMALL, j)

            def squares_of_x(t):
                for n in range(4):
                    act.wait_ge(s_x[n], 16)
                act.activation(XCT[:, :, :].rearrange("p a s -> p (a s)"), GA[:, t, :], ACT.Square,
                               accum_out=SS[:, t:t + 1])
                act.drain().then_inc(s_ss, 1)

            def sines():
                act.wait_ge(s_ang, 1)
                for half, sc in ((0, -1.0), (1, 1.0)):
                    act.activation(TAB[:, 0, :, 64 * half:64 * half + 64], RR[:, 0, :, :], ACT.Sin, scale=sc).then_inc(s_sin, 1)
                    act.activation(TAB[:, 1, :, 64 * half:64 * half + 64], RR[:, 1, :, :], ACT.Sin).then_inc(s_sin, 1)

            def copy_small():
                act.wait_ge(s_mm, 8)
                act.activation(SMT[:, :], acc[0][0][0:SMALL, 0:S], ACT.Copy).then_inc(s_smt, 1)

            def gates_dt():
                act.wait_ge(s_rx, 1)
                act.wait_ge(s_smt, 2)
                act.activation(SM[:, 0, :], acc[0][1][:, 0:SMALL], ACT.Copy, scale=RSX[:, 0:1]).then_inc(s_xa, 1)
                act.wait_ge(s_acc, 1)
                act.activation(SM[:, :, 0:3 * NH], SM[:, :, 0:3 * NH], ACT.Tanh, scale=0.5).then_inc(s_dta, 1)
                act.wait_ge(s_small, 16 * N_SMALL)
                act.activation(ROWS[:, 1, :], ROWS[:, 1, :], ACT.Exp).then_inc(s_dta, 1)

            def softplus():
                act.wait_ge(s_dts, 1)
                act.activation(TM[:, 2, :, :], TM[:, 1, :, :], ACT.Exp, scale=-1.0).then_inc(s_dta, 1)
                act.drain()
                act.activation(TM[:, 3, :, :], TM[:, 2, :, :], ACT.Ln, bias=1.0).then_inc(s_dta, 1)

            def decay_ends():
                act.wait_ge(s_acs, 1)
                act.activation(DAh[:, :, :], DA[:, :, :], ACT.Copy).then_inc(s_dta, 1)
                act.wait_ge(s_dts, 3)
                act.activation(DST[:, :], DST[:, :], ACT.Exp).then_inc(s_dta, 1)
                act.activation(EA1[:, :], ACS[:, 1, :], ACT.Exp).then_inc(s_dta, 1)

            def hidden(n, cnt):
                act.wait_ge(s_hid, cnt)
                act.activation(HT[:, :], X7[:, 0:NG * NCMP], ACT.Tanh, scale=0.5).then_inc(s_hta, 1)

            slots(act, split_hi, C_SMALL, 8, {0: [lambda: squares_of_x(0)], 1: [lambda: squares_of_x(1)], 7: [copy_small]})
            slots(act, split_hi, C_KC, 8, {1: [gates_dt], 2: [softplus], 6: [sines], 7: [lambda: take(C_KC, 1, XR[:, 0, :])]})
            slots(act, split_hi, C_VC, 8, {0: [decay_ends], 2: [lambda: copy_t(E_KC, KV[:, 0:2, :])], 6: [lambda: hidden(0, 1)],
                                           7: [lambda: take(C_VC, 0, XR[:, 0, :])]})
            slots(act, split_hi, C_KS, 8, {2: [lambda: copy_t(E_VC, KV[:, 0:2, :])], 6: [lambda: hidden(1, 4)],
                                           7: [lambda: take(C_KS, 1, XR[:, 0, :])]})
            slots(act, split_hi, C_VS, 8, {2: [lambda: copy_t(E_KS, KT_[:, 0, 0:2, :])],
                                           7: [lambda: take(C_VS, 0, V_(0, 0))]})
            slots(act, split_hi, C_KW, 8, {7: [lambda: take(C_KW, 1, XR[:, 0, :])]})
            slots(act, split_hi, C_VW, 8, {2: [lambda: copy_t(E_KW, KT_[:, 1, 0:2, :])],
                                           7: [lambda: take(C_VW, 0, V_(0, 1))]})

            def exps(n):
                act.wait_ge(s_nm, n + 1)
                for k in range(4):
                    b = k % 2
                    o = PB[:, S * b:S * (b + 1)] if k < 2 else PB[:, 512 + P * b:512 + P * (b + 1)]
                    src = X6[:, S * b:S * (b + 1)] if k < 2 else X7[:, P * b:P * (b + 1)]
                    act.activation(o, src, ACT.Exp, scale=SCALE, bias=NM[:, k:k + 1], accum_out=SUM[:, k:k + 1])
                act.activation(EC[:, :, :], SCB[:, :, :], ACT.Exp).then_inc(s_ex, 1)

            def copy_probs(e):
                act.wait_ge(s_tr, 2 * e + 1)
                act.activation(PTS[:, 0, :], TR[0][:, 0:384], ACT.Copy).then_inc(s_tra, 1)
                act.activation(PTC[:, 0, :], TR[0][0:NCMP, 384:512], ACT.Copy).then_inc(s_tra, 1)

            def head_out(h, e):
                act.wait_ge(s_tr, 2 * e + 2)
                act.activation(LBh[:, ds(h, 1), :], TR[0][:, 0:S].unsqueeze(1), ACT.Copy).then_inc(s_tra, 2)

            def conv(e, m):
                act.wait_ge(s_cw, 2 * m + 2)
                act.wait_ge(s_xs, m + 1)
                for b in range(2):
                    act.wait_ge(s_tr, 2 * e + b + 1)
                    act.activation(TH[:, 2 * b:2 * b + 2, :], TR[b][:, :].rearrange("p (a s) -> p a s", a=2), ACT.Copy)
                    for c in range(2):
                        ct = 2 * b + c
                        x = act.activation(XC[:, ct, :], TR[b][:, c * S:(c + 1) * S], ACT.Identity,
                                           scale=CWs[:, 3, ct:ct + 1], bias=CWs[:, 4, ct:ct + 1])
                    x.then_inc(s_tra, 1)
                    act.drain().then_inc(s_cva, 1)
                act.drain().then_inc(s_trd, 1)

            def conv_tanh(m):
                act.wait_ge(s_cvp, m + 2)
                act.activation(TH[:, :, :], XC[:, :, :], ACT.Tanh).then_inc(s_ct, 1)

            def gate_first(C, par, G, c0):
                take(C, par, G[:, 0, ds(c0, NC)], func=ACT.Tanh, scale=RSX[:, 2:3])

            def gate_second(C, G, c0):
                act.wait_ge(s_acc, C + 1)
                act.activation(G[:, 1, ds(c0, NC)], G[:, 1, ds(c0, NC)], ACT.Tanh, scale=0.5).then_inc(s_gt, 1)

            act.drain().then_inc(s_ex, 1)
            with act.Fori(0, NG) as i:
                C, e = C_AT + 4 * i, E_AT + PER_AT * i
                hk = {7: [lambda: take(C, C_AT % 2, XR[:, 0, :])],
                      SL_Q: [lambda: copy_t(e + EQ, QT(0, 2).rearrange("p (a s) -> p a s", a=2))],
                      15: [lambda: take(C + 1, (C_AT + 1) % 2, XR[:, 0, :])],
                      SL_BC: [lambda: conv(e + EBC, i)],
                      23: [lambda: gate_first(C + 2, C_AT % 2, GA, NC * i)],
                      31: [lambda: gate_first(C + 3, (C_AT + 1) % 2, GB, NC * i),
                           lambda: gate_second(C + 3, GB, NC * i)]}
                for r in range(4):
                    hk.setdefault(SL_PV[r], []).append(lambda r=r: head_out(4 * i + r, e + EPV[r]))
                for r in range(4):
                    hk.setdefault(SL_PT[r], []).append(lambda r=r: copy_probs(e + EPT[r]))
                for r in range(4):
                    hk.setdefault(SL_S[r], []).append(lambda r=r: exps(4 * i + r))
                hk.setdefault(SL_BC + 6, []).append(lambda: conv_tanh(i))
                hk.setdefault(24, []).append(lambda: gate_second(C + 2, GA, NC * i))
                slots(act, split_hi, C, 32, hk)
            with act.Fori(0, 2) as i:
                slots(act, split_hi, C_PA + 2 * i, 16, {})

            def take_z(C, par, t):
                take(C, par, ZR[:, 0, :])
                act.wait_ge(s_acc, C + 1)
                act.activation(ZT[:, :, :], ZR[:, :, :], ACT.Tanh, scale=0.5).then_inc(s_zt, 1)

            def token_rows(e):
                for t in range(2):
                    act.wait_ge(s_tr, 2 * e + t + 1)
                    act.activation(XTOK[:, t, :], TR[t][:, :], ACT.Copy).then_inc(s_tra, 1)

            def scan_exp(g, b):
                act.wait_ge(s_dk, 4 * g + b + 1)
                act.activation(W[:, b, :], X6[:, :], ACT.Exp).then_inc(s_dx, 1)

            def scan_state(g):
                act.wait_ge(s_st, g + 1)
                act.activation(ST[:, :], X7[:, :], ACT.Copy).then_inc(s_stc, 1)

            def scan_squares(g):
                act.wait_ge(s_yg, g + 1)
                for t in range(2):
                    act.activation(W[:, t, :], Y[:, t, :], ACT.Square, accum_out=SS[:, t:t + 1]).then_inc(s_ss, 1)

            def scan_norm(g):
                act.wait_ge(s_pow, g + 2)
                for t in range(2):
                    x = act.activation(Y[:, t, :], Y[:, t, :], ACT.Copy, scale=RS[:, t:t + 1])
                act.drain().then_inc(s_yn, 1)

            def scan_hooks(g, k0):
                return {0: [lambda: scan_exp(g, 0)], 2: [lambda: scan_exp(g, 1)], 3: [lambda: scan_state(g)],
                        4: [lambda: scan_exp(g, 2)], 6: [lambda: scan_exp(g, 3)], 9: [lambda: scan_squares(g)],
                        10: [lambda: scan_norm(g)],
                        12: [lambda: act_split_t(act, g, LBh, k0, NWs, banks=(X6, X7), sm=s_e3, done=s_e3a)]}

            def scan_iteration(C, par, e, m, g=None, k0=None):
                hk = scan_hooks(g, k0) if g is not None else {}
                hk[7] = [lambda: take(C, par, XR[:, 0, :])]
                hk[8] = [lambda: conv(e, m)]
                hk[12] = hk.get(12, []) + [lambda: conv_tanh(m)]
                hk[15] = [lambda: take_z(C + 1, (par + 1) % 2, m), lambda: token_rows(e + 1)]
                slots(act, split_hi, C, 16, hk)

            scan_iteration(C_X0, C_X0 % 2, E_X0, 4)
            with act.Fori(0, 4) as i:
                scan_iteration(C_L1 + 2 * i, C_L1 % 2, E_L1 + 2 * i, 5 + i, i, 4 * i)
            with act.Fori(0, 2) as i:
                slots(act, split_hi, C_PB1 + 2 * i, 16, {})
            with act.Fori(0, 3) as i:
                scan_iteration(C_L2 + 2 * i, C_L2 % 2, E_L2 + 2 * i, 9 + i, i + 4, 4 * i)
            hk = last_hooks(scan_hooks(7, 12))
            hk[15] = [lambda: act_split_t(act, E_PB2, LAh, 0)]
            slots(act, split_hi, C_PB2, 16, hk)
            for n in range(2, 4):
                slots(act, split_hi, C_PB2 + n, 8, {2: [lambda: act_split_t(act, E_PB2 + n - 1, LAh, 4 * n - 4)]})

            def residual_squares(C, n):
                act.wait_ge(s_acc, C + 1)
                for t in range(2):
                    act.activation(XC[:, 2 * t:2 * t + 2, :].rearrange("p a s -> p (a s)"), H[:, t, NC * n:NC * (n + 1)],
                                   ACT.Square, accum_out=SS2[:, t, n:n + 1]).then_inc(s_ss, 1)

            for n in range(4):
                w = COLS[:, CN2 + 4 * n - 4:CN2 + 4 * n]
                slots(act, split_hi, C_WO + n, 8,
                      {2: [lambda: act_split_t(act, E_WO + n - 1, LBh, 4 * n - 4, w) if n else
                           act_split_t(act, E_PB2 + 3, LAh, 12)], 7: [lambda: residual_squares(C_WO + n, n)]})
            act_split_t(act, E_WO + 3, LBh, 12, COLS[:, CN2 + 12:CN2 + 16])
            act.wait_ge(s_pow, 10)

            def mlp(i, last=False):
                C, e = C_MLP + 8 * i, E_MLP + 4 * i
                hk = {}
                for k in range(4):
                    hk[8 * k + 7] = [lambda k=k: take(C + k, (C_MLP + k) % 2, XR[:, 0, :], func=ACT.Relu, scale=RS[:, 2:3])]
                    hk[8 * k + 10] = [lambda k=k: act_split_t(act, e + k, LAh, 4 * k)]
                    if last:
                        hk[8 * k + 39] = [lambda k=k: residual_squares(C + 4 + k, k)]
                slots(act, split_hi, C, 64, hk, last)

            with act.Fori(0, 3) as i:
                mlp(i)
            mlp(3, last=True)
            act.wait_ge(s_pow, 11)
            act.wait_ge(s_hw, 4)
            for n in range(2):
                cols = slice(D // 2 * n, D // 2 * (n + 1))
                act.activation(GB[:, 0, cols], GB[:, 0, cols], ACT.Copy, scale=RS[:, 0:1]).then_inc(s_fin[0], 1)

        @block.vector
        def _(dve):
            def take(C, par, o, xa, n=NC):
                dve.wait_ge(s_xa, xa)
                dve.tensor_scalar(o, acc[par][1][:, 0:n], RSX[:, 1:2], None, ALU.mult).then_inc(s_acc, 1)

            def copy_t(e, o):
                dve.wait_ge(s_tr, 2 * e + 2)
                dve.tensor_copy(o, TR[1][:, :].rearrange("p (a s) -> p a s", a=2)).then_inc(s_trd, 1)

            def rope():
                def hv(x):
                    return x.rearrange("p t (h d) -> p t h d", h=4)
                T2 = XC[:, :, :].rearrange("p a s -> p (a s)").rearrange("p (t n) -> p t n", t=2)
                cos = TAB[:, 1, 0:2, :].unsqueeze(2).broadcast_to([P, 2, 4, P])
                dve.tensor_tensor(hv(Y[:, :, :]), hv(XR[:, :, :]), cos, ALU.mult)
                for o, i_ in ((0, 64), (64, 0)):
                    sin = TAB[:, 0, 0:2, o:o + 64].unsqueeze(2).broadcast_to([P, 2, 4, 64])
                    dve.tensor_tensor(hv(T2)[:, :, :, o:o + 64], hv(XR[:, :, :])[:, :, :, i_:i_ + 64], sin, ALU.mult)
                dve.drain()
                dve.tensor_tensor(Y[:, :, :], Y[:, :, :], T2, ALU.add).then_inc(s_rope, 1)

            dve.wait_ge(s_const, 1)
            dve.tensor_copy(identb[:, :], identf[:, :])
            dve.wait_ge(s_colp, 1)
            dve.tensor_copy(COLS[:, 0:16], X6[:, 0:16])
            dve.drain().then_inc(s_colc, 1)
            for n in range(4):
                dve_split_t(dve, E_U + n, LAh, LAl, 4 * n, COLS[:, CN1 + 4 * n:CN1 + 4 * n + 4], banks=UB[n % 2])
                if n == 1:
                    for j in range(LEAD):
                        split_lo(dve, C_SMALL, j)

            def columns():
                dve.wait_ge(s_colp, 2)
                dve.tensor_copy(COLS[:, 16:CCB], X6[:, 16:CCB])
                dve.tensor_copy(COLS[:, CPK:CPK + 64], X6[:, CPK:CPK + 64])
                dve.tensor_scalar(COLS[:, CCB:CPK], X6[:, CCB:CPK], 0.5, None, ALU.mult)
                dve.drain().then_inc(s_colc, 1)

            two_pi = 2.0 * np.pi
            c1 = 6.28125
            c2 = 1.93500518798828125e-3
            c3 = two_pi - c1 - c2
            lim = 3.1415925

            def angles():
                dve.wait_ge(s_small, 16 * N_SMALL)
                dve.tensor_copy(POS[:, :], POSI[:, :])
                dve.drain()
                dve.tensor_tensor(ANG[:, :, :], ROWS[:, 2, :].unsqueeze(1).broadcast_to([P, 3, SH]),
                                  POS[:, :].unsqueeze(2).broadcast_to([P, 3, SH]), ALU.mult)

            def reduce_angles(f):
                steps = [(KK, ANG, 1.0 / two_pi, 0.25 * f), (KK, KK, 1.0, 12582912.0), (KK, KK, 1.0, -12582912.0)]
                for o, i_, m, ad in steps:
                    dve.drain()
                    dve.tensor_scalar(o[:, :, :], i_[:, :, :], m, ad, ALU.mult, ALU.add)
                r = RR[:, f, :, :]
                for prev, c in ((ANG[:, :, :], c1), (r, c2), (r, c3)):
                    dve.drain()
                    dve.scalar_tensor_tensor(r, KK[:, :, :], -c, prev, ALU.mult, ALU.add)
                dve.drain()
                dve.tensor_scalar(r, r, 0.5 * np.pi * f, None, ALU.add)
                dve.drain()
                dve.tensor_scalar(r, r, lim, -lim, ALU.min, ALU.max)
                if f:
                    dve.drain().then_inc(s_ang, 1)

            def gates_dt():
                dve.wait_ge(s_rx, 1)
                dve.wait_ge(s_xa, 1)
                dve.tensor_scalar(SM[:, 1, :], acc[0][1][:, SMALL:2 * SMALL], RSX[:, 1:2], None, ALU.mult).then_inc(s_acc, 1)
                dve.drain()
                raw_dt = SM[:, :, 3 * NH:SMALL]
                dve.tensor_tensor(TM[:, 0, :, :], raw_dt, ROWS[:, 0, :].unsqueeze(1).broadcast_to([P, 2, SH]), ALU.add)
                dve.drain()
                dve.tensor_scalar(TM[:, 1, :, :], TM[:, 0, :, :], -1.0, None, ALU.mult)
                dve.drain()
                dve.tensor_tensor(TM[:, 1, :, :], TM[:, 0, :, :], TM[:, 1, :, :], ALU.max).then_inc(s_dts, 1)

            def softplus():
                dve.wait_ge(s_dta, 1)
                g = SM[:, :, 0:3 * NH].rearrange("p t (h b) -> p t h b", b=3)
                for o, i_ in ((GR[:, :, 0:2], g[:, 1, :, 1:3]), (GR[:, :, 2:4], g[:, 0, :, 1:3]),
                              (GR[:, :, 4:5], g[:, 0, :, 0:1]), (GR[:, :, 5:6], g[:, 1, :, 0:1])):
                    dve.tensor_scalar(o, i_, 0.5, 0.5, ALU.mult, ALU.add)
                dve.wait_ge(s_dta, 4)
                x0, d, e, ln, m = (TM[:, k, :, :] for k in range(5))
                dve.tensor_scalar(d, e, 1.0, None, ALU.add)
                dve.drain()
                dve.tensor_scalar(d, d, -1.0, None, ALU.add)
                dve.drain()
                dve.tensor_scalar(m, d, 0.0, None, ALU.is_equal)
                dve.drain()
                dve.tensor_tensor(d, d, m, ALU.add)
                dve.tensor_tensor(ln, ln, m, ALU.add)
                dve.drain()
                dve.reciprocal(d, d)
                dve.drain()
                dve.tensor_tensor(ln, ln, d, ALU.mult)
                dve.drain()
                dve.tensor_tensor(ln, ln, e, ALU.mult)
                dve.drain()
                dve.scalar_tensor_tensor(DT[:, :, :], x0, 0.0, ln, ALU.max, ALU.add)
                dve.drain()
                dve.scalar_tensor_tensor(DA[:, :, :], DT[:, :, :], -1.0, ROWS[:, 1, :].unsqueeze(1).broadcast_to([P, 2, SH]),
                                         ALU.mult, ALU.mult).then_inc(s_dts, 1)

            def cumsums():
                dve.wait_ge(s_acs, 1)
                dve.tensor_copy(ACS[:, :, :].rearrange("p t h -> p (t h)"), X6[:, 0:P])
                dve.drain()
                dve.tensor_tensor(DST[:, :], X6[:, P:P + SH], ACS[:, 0, :], ALU.subtract).then_inc(s_dts, 1)

            def low_steps():
                dve.wait_ge(s_dta, 5)
                dve.tensor_tensor(DA[:, :, :], DA[:, :, :], DAh[:, :, :].bitcast(F32), ALU.subtract)

            def blocks(n, e, c):
                copy_t(e, KV[:, 2:4, :])
                dve.wait_ge(s_tra, 2 * e + 2)
                dve.drain()
                q = KV[:, :, :].rearrange("p g (j i) -> p g j i", i=STR)
                for h in range(2):
                    x = dve.tensor_tensor(XP[:, STR * h:STR * (h + 1), :, :].rearrange("p i g j -> p g j i"), q[:, :, h:h + NCMP, :],
                                          COLS[:, c + STR * h:c + STR * (h + 1)].unsqueeze(1).unsqueeze(1).broadcast_to([P, NG, NCMP, STR]),
                                          ALU.add)
                dve.drain().then_inc(s_xp, 1)

            def hidden(n):
                dve.wait_ge(s_hta, n + 1)
                dve.scalar_tensor_tensor(HS[:, :], HT[:, :], 1.0, X7[:, 0:NG * NCMP], ALU.add, ALU.mult).then_inc(s_hs, 1)

            def key_rope():
                n = NG * NCMP
                dve.wait_ge(s_hid, 2)
                dve.tensor_scalar(KCN[:, 0, :], X6[0:n, 0:HD], 0.5, None, ALU.mult)
                dve.drain()
                dve.tensor_tensor(KCN[:, 1, 0:64], KCN[:, 0, 64:128], TAB[0:n, 0, 2, 0:64], ALU.mult)
                dve.tensor_tensor(KCN[:, 1, 64:128], KCN[:, 0, 0:64], TAB[0:n, 0, 2, 64:128], ALU.mult)
                dve.drain()
                dve.tensor_tensor(KCN[:, 0, :], KCN[:, 0, :], TAB[0:n, 1, 2, :], ALU.mult)
                dve.drain()
                dve.tensor_tensor(KCN[:, 0, :], KCN[:, 0, :], KCN[:, 1, :], ALU.add).then_inc(s_kcr, 1)

            def key_copy():
                dve.wait_ge(s_hid, 3)
                dve.tensor_copy(KCT[:, :, :].rearrange("p g j -> p (g j)"), X6[:, P:P + NG * NCMP]).then_inc(s_kcr, 1)

            def value_copy():
                dve.wait_ge(s_hid, 5)
                dve.tensor_scalar(VCB[:, :, :].rearrange("p g d -> p (g d)"), X6[0:NCMP, :], 0.5, None, ALU.mult).then_inc(s_vcd, 1)

            def take_rope(C, par, xa):
                take(C, par, XR[:, 1, :], xa)
                dve.drain()
                rope()

            slots(dve, split_lo, C_SMALL, 8, {})
            slots(dve, split_lo, C_KC, 8, {1: [gates_dt], 2: [columns, angles], 3: [softplus],
                                           4: [lambda: reduce_angles(0)], 5: [lambda: reduce_angles(1)], 6: [cumsums], 7: [lambda: take(C_KC, 1, XR[:, 1, :], C_KC + 1)]})
            slots(dve, split_lo, C_VC, 8, {1: [low_steps], 2: [lambda: blocks(0, E_KC, CPK)], 6: [lambda: hidden(0)],
                                           7: [lambda: take(C_VC, 0, XR[:, 1, :], C_VC + 1)]})
            dve.wait_ge(s_sin, 4)
            slots(dve, split_lo, C_KS, 8, {1: [key_rope], 2: [lambda: blocks(1, E_VC, CPV)], 5: [key_copy],
                                           6: [lambda: hidden(1)], 7: [lambda: take_rope(C_KS, 1, C_KS + 1)]})
            slots(dve, split_lo, C_VS, 8, {1: [value_copy], 2: [lambda: copy_t(E_KS, KT_[:, 0, 2:4, :])],
                                           7: [lambda: take(C_VS, 0, V_(1, 0), C_VS + 1)]})
            slots(dve, split_lo, C_KW, 8, {7: [lambda: take_rope(C_KW, 1, C_KW + 1)]})
            slots(dve, split_lo, C_VW, 8, {2: [lambda: copy_t(E_KW, KT_[:, 1, 2:4, :])],
                                           7: [lambda: take(C_VW, 0, V_(1, 1), C_VW + 1)]})

            def maxima(n):
                dve.wait_ge(s_sc, n + 1)
                dve.tensor_reduce(MX[:, 0:2], X6[:, :].rearrange("p (b k) -> p b k", b=2), AX.X, ALU.max)
                dve.tensor_reduce(MX[:, 2:4], X7[:, 0:S].rearrange("p (b k) -> p b k", b=2), AX.X, ALU.max)
                dve.tensor_tensor(SCB[:, :, :], X7[:, S:S + 2 * NCMP].rearrange("p (t j) -> p t j", t=2), CNEG[:, :, :], ALU.add)
                dve.drain()
                dve.tensor_reduce(MX[:, 4:6], SCB[:, :, :], AX.X, ALU.max)
                dve.drain()
                dve.tensor_scalar(NM[:, :], MX[:, :], -SCALE, None, ALU.mult)
                dve.drain()
                dve.scalar_tensor_tensor(SCB[:, :, :], SCB[:, :, :], SCALE, NM[:, 4:6].unsqueeze(2).broadcast_to([P, 2, NCMP]),
                                         ALU.mult, ALU.add).then_inc(s_nm, 1)

            def scale_probs(n):
                dve.wait_ge(s_ex, n + 2)
                dve.tensor_tensor(EC[:, :, :], EC[:, :, :], CM1[:, :, :], ALU.mult)
                dve.drain()
                dve.tensor_reduce(SUM[:, 4:6], EC[:, :, :], AX.X, ALU.add)
                dve.drain()
                dve.tensor_scalar(SUM[:, :], SUM[:, :], TINY, None, ALU.max)
                dve.drain()
                dve.reciprocal(SUM[:, :], SUM[:, :])
                dve.drain()
                dve.tensor_tensor(SUM[:, :].unsqueeze(1), SUM[:, :].unsqueeze(1), GR[:, ds(n, 1), :], ALU.mult)
                dve.drain()
                for k in range(4):
                    b = k % 2
                    v = PB[:, S * b:S * (b + 1)] if k < 2 else PB[:, 512 + P * b:512 + P * (b + 1)]
                    dve.tensor_scalar(v, v, SUM[:, k:k + 1], None, ALU.mult)
                dve.tensor_tensor(PC[:, :, :], EC[:, :, :], SUM[:, 4:6].unsqueeze(2).broadcast_to([P, 2, NCMP]), ALU.mult)
                dve.drain().then_inc(s_p, 1)

            def copy_probs(e):
                dve.wait_ge(s_tr, 2 * e + 2)
                dve.tensor_copy(PTS[:, 1, :], TR[1][:, 0:384])
                dve.tensor_copy(PTC[:, 1, :], TR[1][0:NCMP, 384:512])
                dve.drain().then_inc(s_trd, 1)

            def head_out(h, e):
                dve.wait_ge(s_tra, 2 * e + 2)
                dve.tensor_tensor(LBl[:, ds(h, 1), :], TR[0][:, 0:S].unsqueeze(1), LBh[:, ds(h, 1), :].bitcast(F32),
                                  ALU.subtract).then_inc(s_trd, 1)

            def taps(m, k):
                dve.wait_ge(s_cva, 2 * m + 2)
                for ct in range(4):
                    dve.scalar_tensor_tensor(XC[:, ct, k:S], TH[:, ct, 0:S - k], CWs[:, 3 - k, ct:ct + 1],
                                             XC[:, ct, k:S], ALU.mult, ALU.add)
                x = dve.drain()
                if k == 3:
                    x.then_inc(s_cvp, 1)

            def conv_out(m, o):
                dve.wait_ge(s_ct, m + 1)
                dve.scalar_tensor_tensor(o, TH[:, :, :], 1.0, XC[:, :, :], ALU.add, ALU.mult).then_inc(s_xs, 1)

            def gate_out(G, c0, n):
                dve.wait_ge(s_gt, n + 1)
                dve.tensor_scalar(G[:, :, ds(c0, NC)], G[:, :, ds(c0, NC)], 0.5, 0.5, ALU.mult, ALU.add)

            dve.drain().then_inc(s_xs, 1)
            dve.drain().then_inc(s_cvp, 1)
            dve.drain().then_inc(s_e3d, 1)
            with dve.Fori(0, NG) as i:
                C, e = C_AT + 4 * i, E_AT + PER_AT * i
                hk = {7: [lambda: take_rope(C, C_AT % 2, C + 1)],
                      SL_Q: [lambda: copy_t(e + EQ, QT(2, 4).rearrange("p (a s) -> p a s", a=2))],
                      15: [lambda: take(C + 1, (C_AT + 1) % 2, XR[:, 1, :], C + 2)],
                      23: [lambda: take(C + 2, C_AT % 2, GA[:, 1, ds(NC * i, NC)], C + 3)],
                      31: [lambda: take(C + 3, (C_AT + 1) % 2, GB[:, 1, ds(NC * i, NC)], C + 4),
                           lambda: gate_out(GB, NC * i, 2 * i + 1)]}
                for r in range(4):
                    hk.setdefault(SL_PV[r], []).append(lambda r=r: head_out(4 * i + r, e + EPV[r]))
                for r in range(4):
                    hk.setdefault(SL_PT[r], []).append(lambda r=r: copy_probs(e + EPT[r]))
                for r in range(4):
                    hk.setdefault(SL_S[r], []).append(lambda r=r: maxima(4 * i + r))
                    hk.setdefault(SL_S[r] + 1, []).append(lambda r=r: scale_probs(4 * i + r))
                for k in (1, 2, 3):
                    hk.setdefault(SL_BC + k, []).append(lambda k=k: taps(i, k))
                hk.setdefault(SL_BC + 8, []).append(lambda: conv_out(i, BCT[:, ds(4 * i, 4), :]))
                hk.setdefault(27, []).append(lambda: gate_out(GA, NC * i, 2 * i))
                slots(dve, split_lo, C, 32, hk)

            def mult_gate(C, par, cols):
                dve.wait_ge(s_mm, 8 * C + 8)
                for t in range(2):
                    x = dve.tensor_tensor(GA[:, t, cols], acc[par][t][:, :], GA[:, t, cols], ALU.mult)
                x.then_inc(s_acc, 1)

            with dve.Fori(0, 2) as i:
                C = C_PA + 2 * i
                slots(dve, split_lo, C, 16, {7: [lambda: mult_gate(C, C_PA % 2, ds(2 * NC * i, NC))],
                                             15: [lambda: mult_gate(C + 1, (C_PA + 1) % 2, ds(2 * NC * i + NC, NC))]})

            def scan_w(g, b):
                dve.wait_ge(s_dx, 4 * g + b + 1)
                dve.tensor_tensor(heads4(W[:, b, :]), heads4(W[:, b, :]),
                                  CBB[:, b // 2, :].unsqueeze(1).broadcast_to([P, 4, P]), ALU.mult).then_inc(s_w, 1)

            def scan_first(g):
                dve.wait_ge(s_cb, g + 1)
                dve.tensor_tensor(CBB[:, 0:2, :], X7[:, 0:2 * P].rearrange("p (c l) -> p c l", c=2),
                                  tri[:, :].unsqueeze(1).broadcast_to([P, 2, P]), ALU.mult)
                dve.tensor_copy(CBB[:, 2, :], X7[:, 2 * P:3 * P]).then_inc(s_cbc, 1)
                dve.wait_ge(s_zt, g + 1)
                dve.scalar_tensor_tensor(ZT[:, :, :], ZT[:, :, :], 1.0, ZR[:, :, :], ALU.add, ALU.mult)
                dve.drain()

            def scan_y0(g):
                dve.wait_ge(s_y0, g + 1)
                dve.wait_ge(s_xdd, 2 * g + 2)
                dve.tensor_tensor(Y[:, 0, :], X7[:, :], XD[:, 0, :], ALU.add).then_inc(s_y0d, 1)

            def scan_y1(g):
                dve.wait_ge(s_ey, g + 1)
                YO = XDT[:, 0, :]
                dve.tensor_tensor(heads8(YO), heads8(X6[:, :]),
                                  EA1[:, ds(8 * g, 8)].unsqueeze(2).broadcast_to([P, 8, SH]), ALU.mult)
                dve.tensor_tensor(Y[:, 1, :], X7[:, :], XD[:, 1, :], ALU.add)
                dve.drain()
                dve.tensor_tensor(Y[:, 1, :], Y[:, 1, :], YO, ALU.add)
                dve.drain()
                dve.scalar_tensor_tensor(Y[:, :, :], Y[:, :, :], 0.5, ZT[:, :, :], ALU.mult, ALU.mult).then_inc(s_yg, 1)

            def scan_hooks(g, k0):
                return {0: [lambda: scan_first(g)], 1: [lambda: scan_w(g, 0)],
                        3: [lambda: scan_w(g, 1)], 5: [lambda: scan_w(g, 2), lambda: scan_y0(g)],
                        7: [lambda: scan_w(g, 3)], 8: [lambda: scan_y1(g)],
                        13: [lambda: dve_split_t(dve, g, LBh, LBl, k0, NWs, banks=(X6, X7), sa=s_e3a, done=s_e3d)]}

            def scan_inputs(t, e):
                dve.wait_ge(s_tra, 2 * e + 2)
                for c in range(2):
                    x = dve.tensor_tensor(heads8(XDT[:, c, :]), heads8(XTOK[:, c, :]),
                                          DT[:, c, ds(8 * t, 8)].unsqueeze(2).broadcast_to([P, 8, SH]), ALU.mult)
                x.then_inc(s_trd, 1)
                dve.drain()
                dve.tensor_tensor(heads8(XDS[:, :]), heads8(XDT[:, 0, :]),
                                  DST[:, ds(8 * t, 8)].unsqueeze(2).broadcast_to([P, 8, SH]), ALU.mult).then_inc(s_xd, 1)

            def scan_iteration(C, par, e, m, xa, t, g=None, k0=None):
                hk = scan_hooks(g, k0) if g is not None else {}
                hk[7] = hk.get(7, []) + [lambda: take(C, par, XR[:, 1, :], xa + 1)]
                hk[9] = hk.get(9, []) + [lambda: taps(m, 1)]
                hk[10] = hk.get(10, []) + [lambda: taps(m, 2)]
                hk[11] = hk.get(11, []) + [lambda: taps(m, 3)]
                hk[12] = [lambda: conv_out(m, XC[:, :, :])]
                hk[15] = [lambda: take(C + 1, (par + 1) % 2, ZR[:, 1, :], xa + 2), lambda: scan_inputs(t, e + 1)]
                slots(dve, split_lo, C, 16, hk)

            def add_gated(groups, par, cols, o, T):
                dve.wait_ge(s_mm, groups)
                for t in range(2):
                    x = dve.tensor_tensor(T[:, t, :], acc[par][t][:, :], GB[:, t, cols], ALU.mult)
                x.then_inc(s_acc, 1)
                dve.drain()
                return dve.tensor_tensor(GA[:, :, cols] if o is None else o[:, :, :], GA[:, :, cols], T[:, 0:2, :], ALU.add)

            scan_iteration(C_X0, C_X0 % 2, E_X0, 4, XA_X0, 0)
            with dve.Fori(0, 4) as i:
                scan_iteration(C_L1 + 2 * i, C_L1 % 2, E_L1 + 2 * i, 5 + i, XA_X0 + 2 + 2 * i, i + 1, i, 4 * i)
            with dve.Fori(0, 2) as i:
                C = C_PB1 + 2 * i
                slots(dve, split_lo, C, 16, {7: [lambda: add_gated(8 * C + 8, C_PB1 % 2, ds(2 * NC * i, NC), None, W[:, 2:4, :])],
                                             15: [lambda: add_gated(8 * C + 16, (C_PB1 + 1) % 2, ds(2 * NC * i + NC, NC), None, W[:, 2:4, :])]})
            with dve.Fori(0, 3) as i:
                scan_iteration(C_L2 + 2 * i, C_L2 % 2, E_L2 + 2 * i, 9 + i, XA_X0 + 10 + 2 * i, i + 5, i + 4, 4 * i)
            def merge(n, groups):
                add_gated(groups, (C_PB2 + n) % 2, slice(NC * n, NC * n + NC), MG[n % 2], MG[n % 2]).then_inc(s_mg, 1)

            hk = last_hooks(scan_hooks(7, 12))
            hk[13] = hk.get(13, []) + [lambda: merge(0, 8 * C_PB2 + 14)]
            hk[15] = [lambda: dve_split_t(dve, E_PB2, LAh, LAl, 0), lambda: merge(1, 8 * C_PB2 + 16)]
            slots(dve, split_lo, C_PB2, 16, hk)
            for n in range(2, 4):
                slots(dve, split_lo, C_PB2 + n, 8, {2: [lambda: dve_split_t(dve, E_PB2 + n - 1, LAh, LAl, 4 * n - 4)],
                                                    7: [lambda: merge(n, 8 * (C_PB2 + n) + 8)]})

            def add_residual(C, par, n):
                dve.wait_ge(s_mm, 8 * C + 8)
                for t in range(2):
                    x = dve.tensor_tensor(H[:, t, NC * n:NC * (n + 1)], acc[par][t][:, :], H[:, t, NC * n:NC * (n + 1)], ALU.add)
                x.then_inc(s_acc, 1)

            dve.wait_ge(s_hr, 32)
            for n in range(4):
                w = COLS[:, CN2 + 4 * n - 4:CN2 + 4 * n]
                slots(dve, split_lo, C_WO + n, 8,
                      {2: [lambda: dve_split_t(dve, E_WO + n - 1, LBh, LBl, 4 * n - 4, w) if n else
                           dve_split_t(dve, E_PB2 + 3, LAh, LAl, 12)],
                       7: [lambda: add_residual(C_WO + n, (C_WO + n) % 2, n)]})
            dve_split_t(dve, E_WO + 3, LBh, LBl, 12, COLS[:, CN2 + 12:CN2 + 16])

            def row_variance(n):
                dve.wait_ge(s_ss, n)
                dve.tensor_reduce(SS[:, 0:2], SS2[:, :, :], AX.X, ALU.add)
                dve.drain()
                dve.tensor_scalar(VV[:, 0:2], SS[:, 0:2], 1.0 / D, EPS, ALU.mult, ALU.add).then_inc(s_v, 1)

            row_variance(SS_WO)
            dve.wait_ge(s_pow, 10)

            def mlp_rows(C, par, xa):
                dve.wait_ge(s_xa, xa)
                dve.tensor_scalar(XR[:, 1, :], acc[par][1][:, :], RS[:, 3:4], 0.0, ALU.mult, ALU.max).then_inc(s_acc, 1)
                dve.drain()
                dve.tensor_tensor(Y[:, :, :], XR[:, :, :], XR[:, :, :], ALU.mult).then_inc(s_ff, 1)

            def weigh(k):
                dve.wait_ge(s_wf, 16)
                dve.drain()
                cols = slice(NC * k, NC * (k + 1))
                dve.tensor_tensor(GB[:, :, cols], H[:, :, cols], GA[:, 0:1, cols].broadcast_to([P, 2, NC]), ALU.mult)
                dve.drain().then_inc(s_hw, 1)

            def mlp(i, last=False):
                C, e = C_MLP + 8 * i, E_MLP + 4 * i
                hk = {}
                for k in range(4):
                    hk[8 * k + 7] = [lambda k=k: mlp_rows(C + k, (C_MLP + k) % 2, XA_UP + 4 * i + k + 1)]
                    hk[8 * k + 10] = [lambda k=k: dve_split_t(dve, e + k, LAh, LAl, 4 * k)]
                    hk[8 * k + 39] = [lambda k=k: add_residual(C + 4 + k, (C_MLP + k) % 2, k)]
                    if last:
                        hk[8 * k + 39].append(lambda k=k: weigh(k))
                slots(dve, split_lo, C, 64, hk, last)

            with dve.Fori(0, 3) as i:
                mlp(i)
            mlp(3, last=True)
            row_variance(SS_WO + 8)
            dve.wait_ge(s_pow, 11)
            for n in range(2):
                cols = slice(D // 2 * n, D // 2 * (n + 1))
                dve.tensor_scalar(GB[:, 1, cols], GB[:, 1, cols], RS[:, 1:2], None, ALU.mult).then_inc(s_fin[1], 1)


_INS = ["x", "positions", "norm_mix_w", "w_in", "cmp_pos_k", "cmp_pos_v", "cmp_k_w1", "cmp_k_w2", "cmp_v_w1",
        "cmp_v_w2", "conv_w", "conv_b", "dt_bias", "a_log", "ssm_d", "ssm_norm_w", "w_proj_nsa", "w_proj_ssm",
        "w_out", "norm_mlp_w", "w_up", "w_down", "norm_final_w"]
_WHOLE = ("x", "positions", "norm_final_w")


def kernel(**inputs):
    import concourse.bacc as bacc
    from concourse.bass_utils import run_bass_kernel_spmd

    nc = bacc.Bacc("TRN2", target_bir_lowering=False, num_devices=1)
    arrays, args = {}, {}
    for name in _INS:
        v = np.ascontiguousarray(inputs[name])
        if name not in _WHOLE:
            v = v[0]
        arrays[name] = v
        args[name] = nc.dram_tensor(name, v.shape, mybir.dt.from_np(v.dtype), kind="ExternalInput").ap()
    inv = (np.float32(10000.0) ** (-np.arange(0, HD, 2, dtype=np.float32) / np.float32(HD))).astype(np.float32)
    arrays["inv_freq"] = inv
    args["inv_freq"] = nc.dram_tensor("inv_freq", inv.shape, F32, kind="ExternalInput").ap()
    out = nc.dram_tensor("out", (1, S, D), F32, kind="ExternalOutput").ap()
    build(nc, args, out)
    r = run_bass_kernel_spmd(nc, [arrays], core_ids=[0])
    return r.results[0]["out"]
```
